# Optimizing a Trainium2 kernel written in Bass

```python
import math
import jax
import jax.numpy as jnp
from jax import lax
import numpy as np

D_MODEL = 1024
BATCH = 1
SEQ = 128
DEPTH = 2
DEC_BATCH = 1
DEC_SEQ = 512
PAST_LEN = 128

GRID_W = 64
HEAD_DIM = 64
DA_HEADS = 4
DA_WIDTH = DA_HEADS * 2 * HEAD_DIM
NA_HEADS = 8
NA_WIDTH = NA_HEADS * HEAD_DIM
NA_ROWS_MAX = 8
NA_COLS = 16
NA_QUERY_COLS = 16
IN_COLS = 3 * DA_WIDTH + 3 * NA_WIDTH + 2 * D_MODEL
ROPE_BASE = 10000.0
ROPE_PAIRS = HEAD_DIM // 4
QUERY_BLOCK = 128
N_EXPERTS = 16
N_GROUPS = 4
EXPERTS_PER_GROUP = N_EXPERTS // N_GROUPS
TOP_K = 2
D_EXPERT = 256
N_MOD = 6
EPS = 1e-6

kernel_name = "hybrid_diffattn_natten_moe_dit_step"

def rms_norm(x, g):
    xf = x.astype(jnp.float32)
    y = xf * lax.rsqrt(jnp.mean(xf * xf, axis=-1, keepdims=True) + EPS)
    return (y * g.astype(jnp.float32)).astype(x.dtype)

def modulation(cond, w_mod, b_mod):
    m = (jax.nn.silu(cond) @ w_mod + b_mod)[..., None, :]
    return jnp.split(m, N_MOD, axis=-1)

def axial_rope_tables(n_tokens):
    t = jnp.arange(n_tokens)
    pos = jnp.stack([t // GRID_W, t % GRID_W], axis=-1).astype(jnp.float32)
    inv_freq = ROPE_BASE ** (-jnp.arange(ROPE_PAIRS, dtype=jnp.float32) / ROPE_PAIRS)
    ang = pos[:, :, None] * inv_freq
    return jnp.cos(ang), jnp.sin(ang)

def apply_axial_rope(x, cos, sin):
    xs = x.reshape(x.shape[:-1] + (2, 2, ROPE_PAIRS))
    x1, x2 = xs[..., 0, :], xs[..., 1, :]
    cos, sin = cos.astype(x.dtype), sin.astype(x.dtype)
    out = jnp.stack([x1 * cos - x2 * sin, x2 * cos + x1 * sin], axis=-2)
    return out.reshape(x.shape)

def split_query_blocks(q, axis):
    n = q.shape[axis]
    q = q.reshape(q.shape[:axis] + (n // QUERY_BLOCK, QUERY_BLOCK) + q.shape[axis + 1:])
    return jnp.moveaxis(q, axis, 0)

def merge_query_blocks(o, axis):
    o = jnp.moveaxis(o, 0, axis)
    return o.reshape(o.shape[:axis] + (o.shape[axis] * o.shape[axis + 1],) + o.shape[axis + 2:])

def diff_attention(q, k, v, lam, scale):
    s = jnp.einsum('bmhqd,bmhkd->bmhqk', q, k).astype(jnp.float32) * scale
    p = jax.nn.softmax(s, axis=-1)
    a = p[:, 0] - lam * p[:, 1]
    return jnp.einsum('bhqk,bhkd->bhqd', a.astype(v.dtype), v)

def dense_attention(q, k, v, scale):
    s = jnp.einsum('bhqd,bhkd->bhqk', q, k).astype(jnp.float32) * scale
    p = jax.nn.softmax(s, axis=-1).astype(v.dtype)
    return jnp.einsum('bhqk,bhkd->bhqd', p, v)

def neighbourhood_attention(q, k, v, k_ctx, v_ctx, rpb, scale):
    B, H, N, DH = q.shape
    rows = N // GRID_W
    kh = min(NA_ROWS_MAX, rows)
    qr = math.gcd(rows, NA_ROWS_MAX)
    qc = NA_QUERY_COLS
    uh = min(kh + qr - 1, rows)
    uw = min(NA_COLS + qc - 1, GRID_W)
    n_rb, n_cb = rows // qr, GRID_W // qc
    q_rows = jnp.arange(n_rb)[:, None] * qr + jnp.arange(qr)
    q_cols = jnp.arange(n_cb)[:, None] * qc + jnp.arange(qc)
    k_rows = jnp.clip(q_rows[:, :1] - kh // 2, 0, rows - uh) + jnp.arange(uh)
    k_cols = jnp.clip(q_cols[:, :1] - NA_COLS // 2, 0, GRID_W - uw) + jnp.arange(uw)
    r0 = jnp.clip(q_rows - kh // 2, 0, rows - kh)
    c0 = jnp.clip(q_cols - NA_COLS // 2, 0, GRID_W - NA_COLS)
    dr = k_rows[:, None, :] - q_rows[:, :, None]
    dc = k_cols[:, None, :] - q_cols[:, :, None]
    row_ok = (k_rows[:, None, :] >= r0[:, :, None]) & (k_rows[:, None, :] < r0[:, :, None] + kh)
    col_ok = (k_cols[:, None, :] >= c0[:, :, None]) & (k_cols[:, None, :] < c0[:, :, None] + NA_COLS)
    ri = jnp.clip(dr + NA_ROWS_MAX - 1, 0, 2 * NA_ROWS_MAX - 2)[:, None, :, None, :, None]
    ci = jnp.clip(dc + NA_COLS - 1, 0, 2 * NA_COLS - 2)[None, :, None, :, None, :]
    ok = row_ok[:, None, :, None, :, None] & col_ok[None, :, None, :, None, :]
    bias = jnp.where(ok, rpb[:, ri, ci].astype(jnp.float32), -jnp.inf)
    bias = jnp.moveaxis(bias.reshape(H, n_rb, n_cb, qr * qc, uh * uw), 1, 0)
    idx = (k_rows[:, None, :, None] * GRID_W + k_cols[None, :, None, :]).reshape(n_rb, n_cb, uh * uw)
    qb = q.reshape(B, H, n_rb, qr, n_cb, qc, DH).transpose(2, 0, 1, 4, 3, 5, 6)
    qb = qb.reshape(n_rb, B, H, n_cb, qr * qc, DH)
    n_loc = uh * uw

    def row_block(args):
        q_blk, idx_blk, bias_blk = args
        kg = jnp.take(k, idx_blk, axis=2)
        vg = jnp.take(v, idx_blk, axis=2)
        s_loc = jnp.einsum('bhcqd,bhckd->bhcqk', q_blk, kg).astype(jnp.float32) * scale + bias_blk
        s_ctx = jnp.einsum('bhcqd,bhkd->bhcqk', q_blk, k_ctx).astype(jnp.float32) * scale
        p = jax.nn.softmax(jnp.concatenate([s_loc, s_ctx], axis=-1), axis=-1).astype(v.dtype)
        return (jnp.einsum('bhcqk,bhckd->bhcqd', p[..., :n_loc], vg)
                + jnp.einsum('bhcqk,bhkd->bhcqd', p[..., n_loc:], v_ctx))

    o = lax.map(row_block, (qb, idx, bias))
    o = o.reshape(n_rb, B, H, n_cb, qr, qc, DH).transpose(1, 2, 0, 4, 3, 5, 6)
    return o.reshape(B, H, N, DH)

def split_projection(p):
    B, N, _ = p.shape
    offs = [DA_WIDTH, 2 * DA_WIDTH, 3 * DA_WIDTH, 3 * DA_WIDTH + NA_WIDTH,
            3 * DA_WIDTH + 2 * NA_WIDTH, 3 * DA_WIDTH + 3 * NA_WIDTH, 3 * DA_WIDTH + 3 * NA_WIDTH + D_MODEL]
    da_q, da_k, da_v, na_q, na_k, na_v, g_a, g_b = jnp.split(p, offs, axis=-1)
    da_q = da_q.reshape(B, N, 2, DA_HEADS, HEAD_DIM).transpose(0, 2, 3, 1, 4)
    da_k = da_k.reshape(B, N, 2, DA_HEADS, HEAD_DIM).transpose(0, 2, 3, 1, 4)
    da_v = da_v.reshape(B, N, DA_HEADS, 2 * HEAD_DIM).transpose(0, 2, 1, 3)
    heads = lambda t: t.reshape(B, N, NA_HEADS, HEAD_DIM).transpose(0, 2, 1, 3)
    return da_q, da_k, da_v, heads(na_q), heads(na_k), heads(na_v), g_a, g_b

def moe(h, w_router, b_router, w_gate, w_up, w_down):
    scores = jax.nn.sigmoid((h @ w_router).astype(jnp.float32))
    sel = scores + b_router.astype(jnp.float32)
    grp = sel.reshape(sel.shape[:-1] + (N_GROUPS, EXPERTS_PER_GROUP))
    grp_score = lax.top_k(grp, 2)[0].sum(-1)
    best = jnp.argmax(grp_score, axis=-1)
    in_group = (jnp.arange(N_EXPERTS) // EXPERTS_PER_GROUP) == best[..., None]
    _, idx = lax.top_k(jnp.where(in_group, sel, -jnp.inf), TOP_K)
    w = jnp.take_along_axis(scores, idx, axis=-1)
    w = w / jnp.sum(w, axis=-1, keepdims=True)
    combine = jnp.sum(jax.nn.one_hot(idx, N_EXPERTS, dtype=jnp.float32) * w[..., None], axis=-2)
    combine = combine.astype(h.dtype)
    out = jnp.zeros_like(h)
    for e in range(N_EXPERTS):
        hid = jax.nn.silu(h @ w_gate[e]) * (h @ w_up[e])
        out = out + combine[..., e:e + 1] * (hid @ w_down[e])
    return out

def trunk_layer(x, cond, lp, lam_init, ctx_kv=None):
    sh1, sc1, gt1, sh2, sc2, gt2 = modulation(cond, lp['w_mod'], lp['b_mod'])
    h = rms_norm(x, lp['g_norm1']) * (1 + sc1) + sh1
    da_q, da_k, da_v, na_q, na_k, na_v, g_a, g_b = split_projection(h @ lp['w_in'])
    da_q, da_k = rms_norm(da_q, lp['g_q_da']), rms_norm(da_k, lp['g_k_da'])
    na_q, na_k = rms_norm(na_q, lp['g_q_na']), rms_norm(na_k, lp['g_k_na'])
    f32 = jnp.float32
    lam = (jnp.exp(jnp.sum(lp['lam_q1'].astype(f32) * lp['lam_k1'].astype(f32)))
           - jnp.exp(jnp.sum(lp['lam_q2'].astype(f32) * lp['lam_k2'].astype(f32))) + lam_init)
    scale = HEAD_DIM ** -0.5
    if ctx_kv is None:
        o_a = merge_query_blocks(lax.map(lambda qq: diff_attention(qq, da_k, da_v, lam, scale),
                                         split_query_blocks(da_q, 3)), 2)
        o_b = merge_query_blocks(lax.map(lambda qq: dense_attention(qq, na_k, na_v, scale),
                                         split_query_blocks(na_q, 2)), 2)
        new_ctx = (da_k, da_v, na_k, na_v)
    else:
        ctx_da_k, ctx_da_v, ctx_na_k, ctx_na_v = ctx_kv
        cos, sin = axial_rope_tables(x.shape[1])
        da_q, da_k = apply_axial_rope(da_q, cos, sin), apply_axial_rope(da_k, cos, sin)
        k_all = jnp.concatenate([da_k, ctx_da_k], axis=3)
        v_all = jnp.concatenate([da_v, ctx_da_v], axis=2)
        o_a = merge_query_blocks(lax.map(lambda qq: diff_attention(qq, k_all, v_all, lam, scale),
                                         split_query_blocks(da_q, 3)), 2)
        o_b = neighbourhood_attention(na_q, na_k, na_v, ctx_na_k, ctx_na_v, lp['rpb'], scale)
        new_ctx = None
    o_a = rms_norm(o_a, lp['g_subln']) * (1.0 - lam_init)
    B, N = x.shape[0], x.shape[1]
    y_a = o_a.transpose(0, 2, 1, 3).reshape(B, N, DA_WIDTH) @ lp['w_br_a']
    y_b = o_b.transpose(0, 2, 1, 3).reshape(B, N, NA_WIDTH) @ lp['w_br_b']
    mixed = (jax.nn.sigmoid(g_a) * y_a + jax.nn.sigmoid(g_b) * y_b) @ lp['w_out']
    x = x + gt1 * mixed
    h2 = rms_norm(x, lp['g_norm2']) * (1 + sc2) + sh2
    x = x + gt2 * moe(h2, lp['w_router'], lp['b_router'], lp['w_gate'], lp['w_up'], lp['w_down'])
    return x, new_ctx

def setup_inputs(seed: int = 0) -> dict:
    key = jax.random.key(seed)
    ks = jax.random.split(key, 32)
    f32 = jnp.float32

    def nrm(k, shape, s=1.0):
        return jax.random.normal(k, shape, f32) * s

    return {
        'x_prompt': nrm(ks[0], (BATCH, SEQ, D_MODEL)),
        'x_sample': nrm(ks[1], (DEC_BATCH, DEC_SEQ, D_MODEL)),
        'cache_da_k': nrm(ks[2], (DEC_BATCH, DEPTH, 2, DA_HEADS, PAST_LEN, HEAD_DIM)),
        'cache_da_v': nrm(ks[3], (DEC_BATCH, DEPTH, DA_HEADS, PAST_LEN, 2 * HEAD_DIM)),
        'cache_na_k': nrm(ks[4], (DEC_BATCH, DEPTH, NA_HEADS, PAST_LEN, HEAD_DIM)),
        'cache_na_v': nrm(ks[5], (DEC_BATCH, DEPTH, NA_HEADS, PAST_LEN, HEAD_DIM)),
        'c': nrm(ks[6], (DEC_BATCH, D_MODEL)),
        'c_ctx': nrm(ks[7], (D_MODEL,)),
        'w_mod': nrm(ks[8], (DEPTH, D_MODEL, N_MOD * D_MODEL), 0.5 * D_MODEL ** -0.5),
        'b_mod': nrm(ks[9], (DEPTH, N_MOD * D_MODEL), 0.01),
        'g_norm1': 1.0 + nrm(ks[10], (DEPTH, D_MODEL), 0.02),
        'g_norm2': 1.0 + nrm(ks[11], (DEPTH, D_MODEL), 0.02),
        'w_in': nrm(ks[12], (DEPTH, D_MODEL, IN_COLS), D_MODEL ** -0.5),
        'g_q_da': 1.0 + nrm(ks[13], (DEPTH, HEAD_DIM), 0.02),
        'g_k_da': 1.0 + nrm(ks[14], (DEPTH, HEAD_DIM), 0.02),
        'g_q_na': 1.0 + nrm(ks[15], (DEPTH, HEAD_DIM), 0.02),
        'g_k_na': 1.0 + nrm(ks[16], (DEPTH, HEAD_DIM), 0.02),
        'lam_q1': nrm(ks[17], (DEPTH, HEAD_DIM), 0.1),
        'lam_k1': nrm(ks[18], (DEPTH, HEAD_DIM), 0.1),
        'lam_q2': nrm(ks[19], (DEPTH, HEAD_DIM), 0.1),
        'lam_k2': nrm(ks[20], (DEPTH, HEAD_DIM), 0.1),
        'g_subln': 1.0 + nrm(ks[21], (DEPTH, 2 * HEAD_DIM), 0.02),
        'rpb': nrm(ks[22], (DEPTH, NA_HEADS, 2 * NA_ROWS_MAX - 1, 2 * NA_COLS - 1), 0.1),
        'w_br_a': nrm(ks[23], (DEPTH, DA_WIDTH, D_MODEL), DA_WIDTH ** -0.5),
        'w_br_b': nrm(ks[24], (DEPTH, NA_WIDTH, D_MODEL), NA_WIDTH ** -0.5),
        'w_out': nrm(ks[25], (DEPTH, D_MODEL, D_MODEL), D_MODEL ** -0.5),
        'w_router': nrm(ks[26], (D_MODEL, N_EXPERTS), D_MODEL ** -0.5),
        'b_router': nrm(ks[27], (N_EXPERTS,), 0.01),
        'w_gate': nrm(ks[28], (DEPTH, N_EXPERTS, D_MODEL, D_EXPERT), D_MODEL ** -0.5),
        'w_up': nrm(ks[29], (DEPTH, N_EXPERTS, D_MODEL, D_EXPERT), D_MODEL ** -0.5),
        'w_down': nrm(ks[30], (DEPTH, N_EXPERTS, D_EXPERT, D_MODEL), D_EXPERT ** -0.5),
    }

def reference(x_prompt, x_sample, cache_da_k, cache_da_v, cache_na_k, cache_na_v, c, c_ctx,
              w_mod, b_mod, g_norm1, g_norm2, w_in, g_q_da, g_k_da, g_q_na, g_k_na,
              lam_q1, lam_k1, lam_q2, lam_k2, g_subln, rpb, w_br_a, w_br_b, w_out,
              w_router, b_router, w_gate, w_up, w_down):
    y_prompt, y_sample = x_prompt, x_sample
    da_ks, da_vs, na_ks, na_vs = [], [], [], []
    for l in range(DEPTH):
        lp = {'w_mod': w_mod[l], 'b_mod': b_mod[l], 'g_norm1': g_norm1[l], 'g_norm2': g_norm2[l],
              'w_in': w_in[l], 'g_q_da': g_q_da[l], 'g_k_da': g_k_da[l], 'g_q_na': g_q_na[l],
              'g_k_na': g_k_na[l], 'lam_q1': lam_q1[l], 'lam_k1': lam_k1[l], 'lam_q2': lam_q2[l],
              'lam_k2': lam_k2[l], 'g_subln': g_subln[l], 'rpb': rpb[l], 'w_br_a': w_br_a[l],
              'w_br_b': w_br_b[l], 'w_out': w_out[l], 'w_router': w_router, 'b_router': b_router,
              'w_gate': w_gate[l], 'w_up': w_up[l], 'w_down': w_down[l]}
        lam_init = 0.8 - 0.6 * math.exp(-0.3 * l)
        y_prompt, (dk, dv, nk, nv) = trunk_layer(y_prompt, c_ctx, lp, lam_init)
        da_ks.append(dk)
        da_vs.append(dv)
        na_ks.append(nk)
        na_vs.append(nv)
        y_sample, _ = trunk_layer(y_sample, c, lp, lam_init,
                                  (cache_da_k[:, l], cache_da_v[:, l], cache_na_k[:, l], cache_na_v[:, l]))
    new_da_k = jnp.stack(da_ks, axis=1)
    new_da_v = jnp.stack(da_vs, axis=1)
    new_na_k = jnp.stack(na_ks, axis=1)
    new_na_v = jnp.stack(na_vs, axis=1)
    return (y_prompt, y_sample, new_da_k, new_da_v, new_na_k, new_na_v)


_drawn_inputs = setup_inputs


def setup_inputs(seed=0):
    import zlib

    import numpy as np

    out = dict(_drawn_inputs(seed))
    spreads = {}
    factors = {'g_norm1': 2.932,
     'g_q_da': 8.0,
     'g_k_da': 2.853,
     'g_q_na': 8.0,
     'g_k_na': 2.742,
     'lam_q1': 4.179,
     'lam_k1': 3.137,
     'lam_k2': 3.903,
     'g_subln': 3.924,
     'rpb': 5.804,
     'cache_da_k': 8.0,
     'cache_da_v': 8.0,
     'cache_na_k': 8.0,
     'cache_na_v': 8.0}
    for name, (base, spread) in spreads.items():
        noise = np.random.default_rng([zlib.crc32(name.encode()), seed]).standard_normal(out[name].shape)
        drawn = base * np.exp(spread * noise) if base else spread * noise
        out[name] = jnp.asarray(drawn.astype(out[name].dtype))
    for name, factor in factors.items():
        out[name] = (out[name] * factor).astype(out[name].dtype)
    return out
```

```python
from contextlib import ExitStack
from itertools import count

import numpy as np

import concourse.bass as bass
from concourse import mybir

ALU = mybir.AluOpType
ACT = mybir.ActivationFunctionType
F32, F32R, BF16, I32 = mybir.dt.float32, mybir.dt.float32r, mybir.dt.bfloat16, mybir.dt.int32
AX = mybir.AxisListType

P = 128
D = 1024
DEPTH = 2
NT = 5
KC = D // P
HD = 64
DA_HEADS, NA_HEADS = 4, 8
GRID_W, ROWS = 64, 8
N_EXP, N_GRP = 16, 4
D_EXP = 256
EPS = 1e-6
SAMPLE, CTX, PROMPT = 0, 512, 640
NKEYS = 768
WIN = 256
WSTART = [0, 64, 192, 256]
WKEYS = WIN + P
NEG = -1.0e30

SLOTS = 6
LOOK = 3
BLOCKS = ([("mod", c) for c in range(4)] + [("w_in", c) for c in range(3)] + [("mod", c) for c in range(4, 8)]
          + [("w_in", c) for c in range(3, 6)] + [("mod", c) for c in range(8, 12)]
          + [x for c in range(2) for x in (("w_in", 6 + c), ("br_a", c), ("w_in", 8 + c), ("br_b", c))]
          + [("w_out", c) for c in range(2)])
KQ = {"mod": 4, "w_in": 4, "br_a": 2, "br_b": 2, "w_out": 4}
UNITS = [(kind, c, k) for kind, c in BLOCKS for k in range(KQ[kind])]
NU = len(UNITS)
FIRST = {}
for _u, (_kind, _c, _k) in enumerate(UNITS):
    FIRST.setdefault((_kind, _c), _u)
IS_SPLIT = [kind != "mod" for kind, _, _ in UNITS]
MOE_TILES = (2 * NT * P + N_EXP * (P - 1)) // P
MU = 6

SLOT_USES = [sum(1 for u in range(NU) if u % SLOTS == s) for s in range(SLOTS)]
SLOT_SPLITS = [sum(1 for u in range(NU) if u % SLOTS == s and IS_SPLIT[u]) for s in range(SLOTS)]
SPLIT_NO = [sum(1 for v in range(u) if v % SLOTS == u % SLOTS and IS_SPLIT[v]) for u in range(NU)]

PJ = [("w_in", c) for c in range(6)] + [x for c in range(2) for x in
      (("w_in", 6 + c), ("br_a", c), ("w_in", 8 + c), ("br_b", c))] + [("w_out", 0), ("w_out", 1)]
PJ_ACT = [b for b in PJ if b[0] == "w_in"]
PJ_DVE = [b for b in PJ if b[0] != "w_in"]

DA_UNITS = [(t, h) for t in range(NT) for h in range(DA_HEADS)]
NA_UNITS = [(t, h) for t in range(NT) for h in range(NA_HEADS)]
TR = ([(("h", t, j), True) for t in range(NT) for j in range(2)]
      + [(("q", t), False) for t in range(NT)] + [(("k", t), False) for t in range(NT)]
      + [(("p", i, j), False) for i, (t, _) in enumerate(DA_UNITS) for j in range(2 if t else 1)]
      + [(("nq", t), False) for t in range(NT)] + [(("nk", t), False) for t in range(NT)]
      + [(("np", i), False) for i in range(len(NA_UNITS))]
      + [(("o", t), True) for t in range(NT)]
      + [(("m", t, j), True) for t in range(NT) for j in range(2)]
      + [(("h2", t, j), False) for t in range(NT) for j in range(2)])
TR_NO = {key: n for n, (key, _) in enumerate(TR)}
TR_SPLIT_NO = {key: sum(1 for _, s in TR[:n] if s) for n, (key, s) in enumerate(TR) if s}

PAR = {}
_at = 0
for _name, _n in (("gq_da", 64), ("gk_da", 64), ("gq_na", 64), ("gk_na", 64), ("lam_q1", 64), ("lam_q2", 64),
                  ("lam_k1", 64), ("lam_k2", 64), ("g_subln", 128), ("lam_init", 1), ("one_less", 1)):
    PAR[_name] = (_at, _at + _n)
    _at += _n
NPAR = _at

MOD_BANK = [7, 1, 4, 0] + 8 * [7]
DVE_CHAIN = 295
ACT_CHAIN = 7


def program(nc, w_stream, w_moe, x_in, c_cols, params, b_mod2, g_norms, da_kc, da_vc, na_kc, na_vc, na_bias,
            w_router, b_router, consts, rope, y_out, dk_out, dv_out, nk_out, nv_out):
    nc.disable_value_cache = True
    ctx = ExitStack()
    with ctx:
        ring_base = (nc.sbuf_base + 63) // 64 * 64
        top = [ring_base]

        def at(name, shape, dt, kb=None):
            size = int(np.prod(shape[1:])) * (2 if dt == BF16 else 4)
            if kb is None:
                off = top[0]
                top[0] += (size + 63) // 64 * 64
            else:
                off = area + int(kb * 1024)
                assert int(kb * 1024) + size <= AREA_KB * 1024, name
            return nc.alloc_sbuf_tensor_at(name, shape, dt, offset=off)

        def sem(name):
            return ctx.enter_context(nc.semaphore(name))

        raw, lo, hi = [], [], []
        for s in range(SLOTS):
            off = top[0]
            raw.append(at(f"raw{s}", [P, 2, 512], F32))
            lo.append(nc.alloc_sbuf_tensor_at(f"lo{s}", [P, 2, 512], F32R, offset=off))
            hi.append(at(f"hi{s}", [P, 2, 512], F32R))
        hT_off = top[0]
        hT_hi = at("hT_hi", [P, KC, NT * P], F32R)
        hT_lo_off = top[0]
        hT_lo = at("hT_lo", [P, KC, NT * P], F32R)
        h2T = nc.alloc_sbuf_tensor_at("h2T", [P, KC, NT * P], F32, offset=hT_off)

        def in_lo(name, shape, dt, kb):
            return nc.alloc_sbuf_tensor_at(name, shape, dt, offset=hT_lo_off + int(kb * 1024))

        xT_hi = in_lo("xT_hi", [P, KC, P], F32R, 0)
        xT_lo = in_lo("xT_lo", [P, KC, P], F32R, 4)
        xg = in_lo("xg", [P, D], F32, 8)
        ysb = in_lo("ysb", [P, D], F32, 12)
        silu_g = in_lo("silu_g", [P, D_EXP], F32, 16)
        hid = in_lo("hid", [P, D_EXP], F32, 17)
        hidT_hi = in_lo("hidT_hi", [P, 2, P], F32R, 18)
        hidT_lo = in_lo("hidT_lo", [P, 2, P], F32R, 19)
        ident = at("ident", [P, P], F32)
        tri_f = at("tri_f", [P, P], F32)
        tri = at("tri", [P, P], BF16)
        ones_b = at("ones_b", [P, P], BF16)
        rope_c = at("rope_c", [P, 4, HD], F32)
        rope_s = at("rope_s", [P, 4, HD], F32)
        par = at("par", [P, NPAR], F32)
        wr = at("wr", [P, KC, N_EXP], F32)
        br_b = at("b_router_sb", [P, N_EXP], F32)
        iota_e = at("iota_e", [P, N_EXP], F32)
        iota_t = at("iota_t", [P, MOE_TILES], F32)
        c_raw = at("c_raw", [P, KC, 2], F32)
        c_act = at("c_act", [P, KC, 2], F32)
        modrow = at("modrow", [2, 4, 512], F32)
        rs_v = at("rs_v", [P, 40], F32)
        rs_0 = at("rs_0", [P, 40], F32)
        rs_t = at("rs_t", [P, 40], F32)
        rs = at("rs", [P, 40], F32)
        ssum = at("ssum", [P, 40], F32)
        o_ssum = at("o_ssum", [P, 20], F32)
        neg_m = at("neg_m", [P, 4], F32)
        z = at("z", [P, 4], F32)
        rz = at("rz", [P, 4], F32)
        lam_s = at("lam_s", [P, 2], F32)
        lam_e = at("lam_e", [P, 2], F32)
        lam_p = at("lam_p", [P, 2 * HD], F32)
        neg_lam = at("neg_lam", [P, 1], F32)
        gsub_s = at("gsub_s", [P, P], F32)
        dummy = at("dummy", [P, 8], F32)
        R = {n: at("r_" + n, [P, NT, N_EXP], F32) for n in
             ("score", "sel", "cand", "oh1", "oh2", "selm", "slot")}
        member = at("member", [P, NT, N_EXP], BF16)
        r_m = {n: at("rm_" + n, [P, NT, 4], F32) for n in ("hi", "hi2", "lo", "a", "gs", "gc", "goh")}
        r_1 = {n: at("r1_" + n, [P, NT], F32) for n in ("m", "s1", "s2", "w1", "w2", "p")}
        slot_f = at("slot_f", [P, 2, NT], F32)
        slot_i = at("slot_i", [P, 2, NT], I32)
        n_tiles = at("n_tiles", [P, N_EXP], F32)
        end_t = at("end_t", [P, N_EXP], F32)
        base_s = at("base_s", [P, N_EXP], F32)
        ecmp = at("ecmp", [P, MOE_TILES, N_EXP], F32)
        etab_f = at("etab_f", [P, MOE_TILES], F32)
        etab = at("etab", [P, MOE_TILES], I32)
        tok_id = at("tok_id", [P, NT], I32)
        tok_id_f = at("tok_id_f", [P, NT], F32)
        tok_zero = at("tok_zero", [P, MOE_TILES + 1], I32)
        tidx = at("tidx", [P, 1], I32)
        area = top[0]
        AREA_KB = 94
        assert area + AREA_KB * 1024 <= nc.sbuf_usable_end, (area, nc.sbuf_usable_end)
        x = at("x", [P, NT, D], F32, 0)
        gt = at("gt", [P, 2, D], F32, 20)
        yg = at("yg", [P, 2, 2, D], F32, 60)
        G = at("G", [P, 2, D], F32, 40)
        sh = at("sh", [P, 2, D], F32, 48)
        gn = at("gn", [P, D], F32, 56)
        hrow = at("hrow", [P, NT, D], F32, 60)
        junk = at("junk", [P, D], F32, 80)
        qT = at("qT", [P, 4, NT * P], F32, 0)
        kT = at("kT", [P, 4, NKEYS], F32, 10)
        v = at("v", [P, 6, 512], F32, 22)
        v_sh = at("v_sh", [P, 3, 512], F32, 34)
        o_a = at("o_a", [P, NT, 512], F32, 40)
        stg = at("stg", [P, 2, NT, 512], F32, 50)
        sq = at("sq", [P, 2, 512], F32, 70)
        rt1 = at("rt1", [P, 512], F32, 74)
        rt2 = at("rt2", [P, 512], F32, 76)
        e_da = at("e_da", [P, 2, 2, 640], F32, 74)
        a_da = at("a_da", [P, 2, 640], F32, 84)
        pT = at("pT", [P, 2, 5, P], F32, 89)
        oTb_hi = at("oTb_hi", [P, 4, NT * P], F32R, 50)
        oTb_lo = at("oTb_lo", [P, 4, NT * P], F32R, 60)
        bias_na = at("bias_na", [P, 2, 2, WKEYS], F32, 74)
        s_na = at("s_na", [P, 2, WKEYS], F32, 80)
        e_na = at("e_na", [P, 2, WKEYS], F32, 83)
        p_na = at("p_na", [P, 2, WKEYS], F32, 86)
        pT_na = at("pT_na", [P, 2, 3, P], F32, 89)
        oTa_hi = at("oTa_hi", [P, 4, NT * P], F32R, 0)
        oTa_lo = at("oTa_lo", [P, 4, NT * P], F32R, 10)
        sg = at("sg", [P, NT, 512], F32, 20)
        mixed = at("mixed", [P, NT, D], F32, 70)
        tmp = at("tmp", [P, 2, 512], F32, 90)

        x_spill = nc.dram_tensor("x_spill", [P, NT, D], F32, kind="Internal").ap()
        mod_d = nc.dram_tensor("mod_d", [DEPTH, 2, 6 * D], F32, kind="Internal").ap()
        h_d = nc.dram_tensor("h_d", [NT * P, D], F32, kind="Internal").ap()
        tok_d = nc.dram_tensor("tok_d", [(MOE_TILES + 1) * P, 1], I32, kind="Internal").ap()
        ye_d = nc.dram_tensor("ye_d", [MOE_TILES * P, D], F32, kind="Internal").ap()

        ps = ctx.enter_context(nc.psum_tensor("ps", [P, 8, 512], F32))
        ps_flat = ps[:].rearrange("p b n -> p (b n)")

        class Signal:

            def __init__(self, name, n, m=0, unit=1, start=0):
                self.sem, self.name, self.n, self.m, self.unit, self.start = sem(name), name, n, m, unit, start
                self.layer = (n + m * MOE_TILES) * unit

            def at(self, l, k, i=None):
                val = l * self.layer + ((k + 1) * self.unit + self.start)
                return val if i is None else val + self.n * self.unit + i * (self.m * self.unit)

        loaded = [Signal(f"w_loaded{s}", SLOT_USES[s], 1, 16) for s in range(SLOTS)]
        is_hi = [Signal(f"w_hi{s}", SLOT_SPLITS[s], 1) for s in range(SLOTS)]
        is_lo = [Signal(f"w_lo{s}", SLOT_SPLITS[s], 1) for s in range(SLOTS)]
        used = [Signal(f"w_used{s}", SLOT_USES[s], 1, 1, 1) for s in range(SLOTS)]
        s_const = sem("const_loaded")
        s_settled = sem("settled")
        s_x = sem("x_loaded")
        s_zero = sem("zero_tokens")
        s_zeroed = sem("tokens_zeroed")
        s_cact = sem("silu_c")
        s_tri = sem("tri_cast")
        s_modini = sem("mod_bias")
        dve_chain = Signal("dve_chain", DVE_CHAIN)
        act_chain = Signal("act_chain", ACT_CHAIN)
        modrow_ready = Signal("modrow_ready", 12)
        mod_stored = Signal("mod_stored", 12, 0, 16)
        par_loaded = Signal("par_loaded", 1, 0, 16)
        nmod_loaded = Signal("norm_mod_loaded", 6, 0, 16)
        shift_loaded = Signal("shift_loaded", 4, 0, 16)
        gate_loaded = Signal("gate_loaded", 4, 0, 16)
        lam_sum = Signal("lam_sum", 1)
        lam_exp = Signal("lam_exp", 1)
        xsq_done = Signal("xsq_done", 2 * NT)
        rs_in = Signal("rs_in", 7)
        rs_out = Signal("rs_out", 7)
        h_ready = Signal("h_ready", 2 * NT)
        x_spilled = Signal("x_spilled", 1, 0, 16)
        x_back = Signal("x_back", 1, 0, 16)
        tr_done = Signal("tr_done", len(TR))
        tr_act = Signal("tr_act", len(TR))
        tr_dve = Signal("tr_dve", len(TR_SPLIT_NO))
        pj_done = Signal("pj_done", (NT - 1) * len(PJ))
        pj_act = Signal("pj_act", NT * len(PJ_ACT))
        pj_dve = Signal("pj_dve", NT * len(PJ_DVE))
        sum_ready = Signal("sum_ready", 4 * NT)
        qk_ready = Signal("qk_ready", 4 * NT)
        ctx_k = Signal("ctx_k", 2, 0, 16)
        ctx_v = Signal("ctx_v", 2, 0, 16)
        kv_out = Signal("kv_out", 4, 0, 16)
        v_shifted = Signal("v_shifted", 2, 0, 16)
        sc_done = Signal("sc_done", 2 * len(DA_UNITS))
        mx_done = Signal("mx_done", 2 * len(DA_UNITS))
        ex_done = Signal("ex_done", 2 * len(DA_UNITS))
        cb_done = Signal("cb_done", len(DA_UNITS))
        av_done = Signal("av_done", NT)
        oc_done = Signal("oc_done", NT)
        oss_done = Signal("oss_done", NT)
        oa_ready = Signal("oa_ready", NT)
        bias_ld = [Signal(f"bias_ld{b}", 8, 0, 16) for b in range(2)]
        nsc_done = Signal("nsc_done", len(NA_UNITS))
        nmx_done = Signal("nmx_done", len(NA_UNITS))
        nex_done = Signal("nex_done", len(NA_UNITS))
        np_done = Signal("np_done", len(NA_UNITS))
        nav_done = Signal("nav_done", NT)
        nob_hi = Signal("nob_hi", NT)
        nob_done = Signal("nob_done", NT)
        mixed_ready = Signal("mixed_ready", NT)
        xu_done = Signal("xu_done", NT)
        rt_done = Signal("rt_done", 1)
        tanh_done = Signal("tanh_done", 1)
        member_ready = Signal("member_ready", 1)
        pos_done = Signal("pos_done", 1)
        slot_ready = Signal("slot_ready", 1)
        etab_ready = Signal("etab_ready", 1)
        h_stored = Signal("h_stored", NT, 0, 16)
        tidx_loaded = Signal("tidx_loaded", 1, 1, 16)
        scattered = Signal("scattered", 2 * NT, 0, 16)
        xg_loaded = Signal("xg_loaded", 0, 1, 16)
        xt_done = Signal("xt_done", 0, 2)
        xt_hi = Signal("xt_hi", 0, 2)
        xt_lo = Signal("xt_lo", 0, 2)
        silu_done = Signal("silu_done", 0, 1)
        hid_done = Signal("hid_done", 0, 1)
        ht_done = Signal("ht_done", 0, 1)
        ht_hi = Signal("ht_hi", 0, 1)
        ht_lo = Signal("ht_lo", 0, 1)
        y_act = Signal("y_act", 0, 1)
        y_dve = Signal("y_dve", 0, 1)
        y_stored = Signal("y_stored", 0, 1, 16)
        gathered = [Signal(f"gathered{b}", 2 * (3 - b), 0, 16) for b in range(2)]
        x_ready = Signal("x_ready", NT, 0, 1, NT)
        s_out = sem("out_stored")

        def sums(l, kind, t):
            if t < NT - 1:
                return pj_done.sem, pj_done.at(l, PJ.index(kind) * (NT - 1) + t)
            u = FIRST[kind] + KQ[kind[0]] - 1
            return used[u % SLOTS].sem, used[u % SLOTS].at(l, u // SLOTS)

        blk = ctx.enter_context(nc.Block())
        uslot = [u % SLOTS for u in range(NU)]
        GI = lambda c: 0 if c == 0 else 1

        def gain(name, heads=8):
            a, b = PAR[name]
            return par[:, a:b].unsqueeze(1).to_broadcast([P, heads, b - a])

        @blk.sync
        def _(sp):
            for s in range(SLOTS):
                sp.sem_inc(used[s].sem, 1)
            with sp.Fori(0, DEPTH) as l:
                full = NU // SLOTS
                with sp.Fori(0, full) as g:
                    for s in range(SLOTS):
                        sp.wait_ge(used[s].sem, l * used[s].layer + g + 1)
                        sp.dma_start(raw[s][:], w_stream[l, g * SLOTS + s]).then_inc(loaded[s].sem, 16)
                for u in range(full * SLOTS, NU):
                    s = uslot[u]
                    sp.wait_ge(used[s].sem, l * used[s].layer + full + 1)
                    sp.dma_start(raw[s][:], w_stream[l, u]).then_inc(loaded[s].sem, 16)
                for t in range(NT):
                    sp.wait_ge(h_ready.sem, h_ready.at(l, NT + t))
                    sp.dma_start(h_d[t * P:(t + 1) * P, :], hrow[:, t, :]).then_inc(h_stored.sem, 16)
                sp.wait_ge(etab_ready.sem, etab_ready.at(l, 0))
                sp.sem_inc(s_settled, 1)

                def gate_up(i, e):
                    for s in range(4):
                        sp.wait_ge(used[s].sem, used[s].at(l, SLOT_USES[s] - 1) + i)
                        sp.dma_start(raw[s][:], w_moe[l, e, s]).then_inc(loaded[s].sem, 16)

                def down(i, e):
                    for s in range(4, MU):
                        sp.wait_ge(used[s].sem, used[s].at(l, SLOT_USES[s] - 1) + i)
                        sp.dma_start(raw[s][:], w_moe[l, e, s]).then_inc(loaded[s].sem, 16)

                def expert(i):
                    return sp.value_load(etab[0:1, bass.ds(i, 1)], min_val=0, max_val=N_EXP - 1)

                gate_up(0, expert(0))
                with sp.Fori(1, MOE_TILES) as i:
                    gate_up(i, expert(i))
                    down(i - 1, expert(i - 1))
                down(MOE_TILES - 1, expert(MOE_TILES - 1))

        @blk.gpsimd
        def _(po):
            po.dma_start(mod_d[:, :, :], b_mod2).then_inc(s_modini, 16)
            for dst, src in ((c_raw[:], c_cols), (ident[:], consts[0]), (tri_f[:], consts[1]),
                             (rope_c[:], rope[0]), (rope_s[:], rope[1]),
                             (wr[:], w_router), (br_b[:], b_router.partition_broadcast(P)),
                             (iota_e[:], consts[2][:, 0:N_EXP]), (iota_t[:], consts[2][:, N_EXP:N_EXP + MOE_TILES]),
                             (tok_id_f[:], consts[2][:, N_EXP + MOE_TILES:N_EXP + MOE_TILES + NT])):
                po.dma_start(dst, src).then_inc(s_const, 16)
            po.wait_ge(s_zero, 1)
            po.dma_start(tok_d.rearrange("(p t) o -> p (t o)", p=P), tok_zero[:]).then_inc(s_zeroed, 16)
            po.wait_ge(s_zeroed, 16)
            po.wait_ge(s_modini, 16)
            with po.Fori(0, DEPTH) as l:
                po.dma_start(par[:], params[l].partition_broadcast(P)).then_inc(par_loaded.sem, 16)

                def store_mod(c):
                    po.wait_ge(modrow_ready.sem, modrow_ready.at(l, c))
                    po.sem_inc(s_settled, 1)
                    po.dma_start(mod_d[l, :, c * 512:(c + 1) * 512], modrow[:, c % 4, :],
                                 accum_op=ALU.add).then_inc(mod_stored.sem, 16)

                def load_vec(dst, which, cond, s):
                    po.dma_start(dst, mod_d[l, cond, which * D:(which + 1) * D].partition_broadcast(P)).then_inc(s.sem, 16)

                def norm_vecs(k):
                    for cond in range(2):
                        load_vec(G[:, cond, :], 3 * k + 1, cond, nmod_loaded)
                    po.dma_start(gn[:], g_norms[k, l].partition_broadcast(P)).then_inc(nmod_loaded.sem, 16)
                    for cond in range(2):
                        load_vec(sh[:, cond, :], 3 * k, cond, shift_loaded)

                for c in range(4):
                    store_mod(c)
                po.wait_ge(mod_stored.sem, mod_stored.at(l, 3))
                po.sem_inc(s_settled, 1)
                norm_vecs(0)
                po.wait_ge(x_ready.sem, x_ready.at(l, -1))
                po.sem_inc(s_settled, 1)
                po.dma_start(x_spill, x[:]).then_inc(x_spilled.sem, 16)
                po.wait_ge(h_ready.sem, h_ready.at(l, NT - 1))
                po.wait_ge(x_spilled.sem, x_spilled.at(l, 0))
                po.sem_inc(s_settled, 1)
                po.dma_start(kT[:, :, CTX:CTX + P], da_kc[l]).then_inc(ctx_k.sem, 16)
                po.dma_start(v[:, 4, :], da_vc[l]).then_inc(ctx_v.sem, 16)
                po.wait_ge(qk_ready.sem, qk_ready.at(l, NT))
                po.sem_inc(s_settled, 1)
                po.dma_start(dk_out[0, l].rearrange("m h s d -> s (m h) d"),
                             stg[:, 1, 0, :].rearrange("p (a d) -> p a d", d=HD)).then_inc(kv_out.sem, 16)
                po.wait_ge(pj_act.sem, pj_act.at(l, NT * 2))
                po.sem_inc(s_settled, 1)
                po.dma_start(dv_out[0, l].rearrange("h s d -> s h d"),
                             v[:, 5, :].rearrange("p (h d) -> p h d", h=DA_HEADS)).then_inc(kv_out.sem, 16)
                for c in range(4, 8):
                    store_mod(c)
                po.wait_ge(kv_out.sem, kv_out.at(l, 1))
                po.wait_ge(sc_done.sem, sc_done.at(l, 2 * len(DA_UNITS) - 1))
                po.sem_inc(s_settled, 1)
                po.dma_start(kT[:, :, CTX:CTX + P], na_kc[l]).then_inc(ctx_k.sem, 16)
                po.wait_ge(av_done.sem, av_done.at(l, NT - 1))
                po.sem_inc(s_settled, 1)
                po.dma_start(v[:, 4, :], na_vc[l]).then_inc(ctx_v.sem, 16)
                po.wait_ge(qk_ready.sem, qk_ready.at(l, 3 * NT))
                po.sem_inc(s_settled, 1)
                po.dma_start(nk_out[0, l].rearrange("h s d -> s h d"),
                             stg[:, 1, 0, :].rearrange("p (a d) -> p a d", d=HD)).then_inc(kv_out.sem, 16)
                po.wait_ge(pj_act.sem, pj_act.at(l, NT * 6 - 1))
                po.sem_inc(s_settled, 1)
                po.dma_start(nv_out[0, l].rearrange("h s d -> s h d"),
                             v[:, 5, :].rearrange("p (h d) -> p h d", h=NA_HEADS)).then_inc(kv_out.sem, 16)
                po.dma_start(v_sh[0:64, :, :], v[64:128, 0:3, :]).then_inc(v_shifted.sem, 16)
                po.dma_start(v_sh[64:128, :, :], v[0:64, 1:4, :]).then_inc(v_shifted.sem, 16)
                for j in range(16):
                    if j == 0:
                        po.wait_ge(kv_out.sem, kv_out.at(l, 3))
                        po.sem_inc(s_settled, 1)
                    if j < 2:
                        po.wait_ge(qk_ready.sem, qk_ready.at(l, 4 * NT - 1))
                        po.sem_inc(s_settled, 1)
                    else:
                        po.wait_ge(nmx_done.sem, nmx_done.at(l, NA_HEADS + 2 * (j - 2) + 1))
                        po.sem_inc(s_settled, 1)
                    po.dma_start(bias_na[:, j % 2, :, :], na_bias[l, j]).then_inc(bias_ld[j % 2].sem, 16)
                for c in range(8, 12):
                    store_mod(c)
                po.wait_ge(mixed_ready.sem, mixed_ready.at(l, NT - 1))
                po.sem_inc(s_settled, 1)
                po.dma_start(x[:], x_spill).then_inc(x_back.sem, 16)
                po.wait_ge(mod_stored.sem, mod_stored.at(l, 11))
                po.sem_inc(s_settled, 1)
                for cond in range(2):
                    load_vec(gt[:, cond, :], 2, cond, gate_loaded)
                norm_vecs(1)
                po.wait_ge(xu_done.sem, xu_done.at(l, NT - 1))
                po.sem_inc(s_settled, 1)
                for cond in range(2):
                    load_vec(gt[:, cond, :], 5, cond, gate_loaded)
                po.wait_ge(slot_ready.sem, slot_ready.at(l, 0))
                po.sem_inc(s_settled, 1)
                for j in range(2):
                    for t in range(NT):
                        po.indirect_dma_start(tok_d, bass.IndirectOffsetOnAxis(slot_i[:, j, t:t + 1], 0),
                                              tok_id[:, t:t + 1], None).then_inc(scattered.sem, 16)
                po.wait_ge(scattered.sem, scattered.at(l, 2 * NT - 1))
                po.sem_inc(s_settled, 1)

                def load_tokens(i):
                    po.dma_start(tidx[:], tok_d[bass.ds(i * P, P), :]).then_inc(tidx_loaded.sem, 16)

                def load_rows(i):
                    po.wait_ge(tidx_loaded.sem, tidx_loaded.at(l, -1, i))
                    po.sem_inc(s_settled, 1)
                    po.indirect_dma_start(xg[:], None, h_d, bass.IndirectOffsetOnAxis(tidx[:, 0:1], 0)).then_inc(
                        xg_loaded.sem, 16)
                    po.wait_ge(xg_loaded.sem, xg_loaded.at(l, 0, i))
                    po.sem_inc(s_settled, 1)
                    load_tokens(i + 1)

                load_tokens(0)
                po.wait_ge(h_stored.sem, h_stored.at(l, NT - 1))
                po.wait_ge(tr_act.sem, tr_act.at(l, len(TR) - 1))
                po.sem_inc(s_settled, 1)

                def store_rows(i):
                    po.wait_ge(y_act.sem, y_act.at(l, 0, i))
                    po.wait_ge(y_dve.sem, y_dve.at(l, 0, i))
                    po.sem_inc(s_settled, 1)
                    po.dma_start(ye_d[bass.ds(i * P, P), :], ysb[:]).then_inc(y_stored.sem, 16)

                def load_after(i):
                    po.wait_ge(xt_done.sem, xt_done.at(l, 1, i - 1))
                    po.sem_inc(s_settled, 1)
                    load_rows(i)

                load_rows(0)
                load_after(1)
                load_after(2)
                with po.Fori(1, MOE_TILES - 2) as i:
                    load_after(i + 2)
                    store_rows(i - 1)
                for i in range(MOE_TILES - 3, MOE_TILES):
                    store_rows(i)
                po.wait_ge(y_stored.sem, y_stored.at(l, 0, MOE_TILES - 1))
                po.sem_inc(s_settled, 1)
                for t in range(NT):
                    if t >= 2:
                        po.wait_ge(x_ready.sem, x_ready.at(l, t - 2))
                        po.sem_inc(s_settled, 1)
                    for j in range(2):
                        po.indirect_dma_start(
                     yg[:, t % 2, j, :], None, ye_d,
                     bass.IndirectOffsetOnAxis(slot_i[:, j, t:t + 1], 0)).then_inc(gathered[t % 2].sem, 16)
            po.wait_ge(x_ready.sem, x_ready.layer * DEPTH + NT)
            po.dma_start(y_out, x[:]).then_inc(s_out, 16)
            po.wait_ge(s_out, 16)
            for s in (kv_out, mod_stored, scattered, y_stored, x_spilled, h_stored):
                po.wait_ge(s.sem, s.layer * DEPTH)

        @blk.scalar
        def _(act):
            act.wait_ge(s_const, 160)
            act.dma_start(x[:], x_in).then_inc(s_x, 16)
            act.activation(c_act[:], c_raw[:], ACT.Silu).then_inc(s_cact, 1)
            with act.Fori(0, DEPTH) as l:

                def split_hi(s, n, i=None):
                    act.wait_ge(loaded[s].sem, loaded[s].at(l, n, i))
                    act.activation(hi[s][:], raw[s][:], ACT.Copy).then_inc(is_hi[s].sem, 1)

                def ahead(u):
                    w = u + LOOK
                    if w < NU and IS_SPLIT[w]:
                        split_hi(uslot[w], w // SLOTS)

                def rs_stage(k):
                    act.wait_ge(rs_in.sem, rs_in.at(l, k))
                    ins = act.activation(rs_0[:], rs_v[:], ACT.Ln)
                    ins.then_inc(act_chain.sem, 1)
                    act.wait_ge(act_chain.sem, act_chain.at(l, k))
                    act.activation(rs_0[:], rs_0[:], ACT.Exp, scale=-0.5).then_inc(rs_out.sem, 1)

                def evac(key, dst):
                    n = TR_NO[key]
                    act.wait_ge(tr_done.sem, tr_done.at(l, n))
                    cols = dst.shape[1] * dst.shape[2]
                    src = ps[:, 5 + n % 2, 0:cols].rearrange("p (a b) -> p a b", b=P)
                    act.activation(dst, src, ACT.Copy).then_inc(tr_act.sem, 1)

                def square_x(k):
                    for t in range(NT):
                        if k == 0:
                            act.wait_ge(x_ready.sem, x_ready.at(l, t - NT))
                        else:
                            act.wait_ge(xu_done.sem, xu_done.at(l, t))
                        if t >= 1:
                            act.wait_ge(xsq_done.sem, xsq_done.at(l, k * NT + t - 1))
                        act.activation(junk[:], x[:, t, :], ACT.Square,
                                       accum_out=ssum[:, t:t + 1]).then_inc(xsq_done.sem, 1)

                for c in range(4):
                    u = FIRST[("mod", c)] + 3
                    act.wait_ge(used[u % SLOTS].sem, used[u % SLOTS].at(l, u // SLOTS))
                    act.activation(modrow[:, c, :], ps[0:2, MOD_BANK[c], :], ACT.Copy).then_inc(modrow_ready.sem, 1)
                square_x(0)
                rs_stage(0)
                act.wait_ge(lam_sum.sem, lam_sum.at(l, 0))
                act.activation(lam_e[:], lam_s[:], ACT.Exp).then_inc(lam_exp.sem, 1)
                for u in range(16):
                    ahead(u)
                for t in range(NT):
                    for j in range(2):
                        evac(("h", t, j), hT_hi[:, 4 * j:4 * j + 4, t * P:(t + 1) * P])

                def qkv(first, names, rs_k):
                    for b in range(3):
                        u0 = FIRST[("w_in", first + b)]
                        for u in range(u0, u0 + 4):
                            ahead(u)
                        for t in range(NT):
                            bank = ps[:, t, :]
                            act.wait_ge(*sums(l, ("w_in", first + b), t))
                            if b < 2:
                                e = (first // 3 * 2 + b) * NT + t
                                if e >= 2:
                                    act.wait_ge(sum_ready.sem, sum_ready.at(l, e - 2))
                                if first == 3 and b == 0 and t == 0:
                                    act.wait_ge(oss_done.sem, oss_done.at(l, NT - 1))
                                if b == 1 and t == 0 and first == 3:
                                    act.wait_ge(kv_out.sem, kv_out.at(l, 1))
                                act.activation(sq[:, t % 2, :], bank, ACT.Square)
                                act.activation(stg[:, b, t, :], bank, ACT.Copy).then_inc(pj_act.sem, 1)
                            else:
                                act.activation(v[:, 5 if t == 0 else t - 1, :], bank, ACT.Copy).then_inc(pj_act.sem, 1)
                        if b < 2:
                            rs_stage(rs_k + b)
                        if b >= 1:
                            name, dst = (names[0], qT) if b == 1 else (names[1], kT)
                            if b == 1 and first == 0:
                                act.wait_ge(x_spilled.sem, x_spilled.at(l, 0))
                            if b == 1 and first == 3:
                                act.wait_ge(kv_out.sem, kv_out.at(l, 1))
                            for t in range(NT):
                                col = t * P if b == 1 else (PROMPT if t == 0 else (t - 1) * P)
                                evac((name, t), dst[:, :, col:col + P])

                qkv(0, ("q", "k"), 1)
                def da_exp(i, m):
                    nk = P if DA_UNITS[i][0] == 0 else 640
                    act.wait_ge(mx_done.sem, mx_done.at(l, 2 * i + m))
                    if i >= 2:
                        act.wait_ge(cb_done.sem, cb_done.at(l, i - 2))
                    act.activation(e_da[:, i % 2, m, 0:nk], ps_flat[:, m * 1024:m * 1024 + nk],
                                   ACT.Exp, bias=neg_m[:, 2 * (i % 2) + m:2 * (i % 2) + m + 1],
                                   accum_out=z[:, 2 * (i % 2) + m:2 * (i % 2) + m + 1]).then_inc(ex_done.sem, 1)

                for i in range(len(DA_UNITS) + 1):
                    if 4 <= i < 20:
                        ahead(FIRST[("mod", 4)] + i - 4)
                    if i < len(DA_UNITS):
                        da_exp(i, 0)
                    if i >= 1:
                        tp, b = DA_UNITS[i - 1][0], (i - 1) % 2
                        if tp == 0:
                            evac(("p", i - 1, 0), pT[:, b, 0:1, :])
                        else:
                            evac(("p", i - 1, 0), pT[:, b, 0:4, :])
                            evac(("p", i - 1, 1), pT[:, b, 4:5, :])
                    if i < len(DA_UNITS):
                        da_exp(i, 1)
                    if i >= 1:
                        t, h = DA_UNITS[i - 1]
                        if h == DA_HEADS - 1:
                            act.wait_ge(av_done.sem, av_done.at(l, t))
                            if t >= 1:
                                act.wait_ge(oss_done.sem, oss_done.at(l, t - 1))
                            act.activation(sq[:, 0, :], ps[:, 4, :], ACT.Square)
                            act.activation(o_a[:, t, :], ps[:, 4, :], ACT.Copy).then_inc(oc_done.sem, 1)
                rs_stage(3)
                qkv(3, ("nq", "nk"), 4)
                for i in range(len(NA_UNITS) + 2):
                    if i % 2 == 0 and i < 32:
                        ahead(FIRST[("mod", 8)] + i // 2)
                    if i < len(NA_UNITS):
                        t, h = NA_UNITS[i]
                        nk = P if t == 0 else WKEYS
                        act.wait_ge(nmx_done.sem, nmx_done.at(l, i))
                        if i >= 2:
                            act.wait_ge(np_done.sem, np_done.at(l, i - 2))
                        src = ps[:, i % 4, 0:nk] if t == 0 else s_na[:, i % 2, :]
                        act.activation(e_na[:, i % 2, 0:nk], src, ACT.Exp, bias=neg_m[:, i % 2:i % 2 + 1],
                                       accum_out=z[:, i % 2:i % 2 + 1]).then_inc(nex_done.sem, 1)
                    if 1 <= i <= len(NA_UNITS):
                        t, h = NA_UNITS[i - 1]
                        evac(("np", i - 1), pT_na[:, (i - 1) % 2, 0:(1 if t == 0 else 3), :])
                    if i >= 2:
                        t, h = NA_UNITS[i - 2]
                        if h == NA_HEADS - 1:
                            act.wait_ge(nav_done.sem, nav_done.at(l, t))
                            act.activation(oTb_hi[:, :, t * P:(t + 1) * P],
                                           ps[:, 4, :].rearrange("p (a b) -> p a b", b=P), ACT.Copy).then_inc(nob_hi.sem, 1)
                for c in range(2):
                    for which, kind in enumerate((("w_in", 6 + c), ("br_a", c), ("w_in", 8 + c), ("br_b", c))):
                        for u in range(FIRST[kind], FIRST[kind] + KQ[kind[0]]):
                            ahead(u)
                        if kind[0] == "w_in":
                            for t in range(NT):
                                act.wait_ge(*sums(l, kind, t))
                                if which == 2 or c == 1:
                                    act.wait_ge(pj_dve.sem, pj_dve.at(l, (PJ_DVE.index(("br_a", c) if which == 2 else ("br_b", c - 1)))
                                           * NT + t))
                                act.activation(sg[:, t, :], ps[:, t, :], ACT.Sigmoid).then_inc(pj_act.sem, 1)
                        if c == 0 and which == 0:
                            for t in range(NT):
                                evac(("o", t), oTa_hi[:, :, t * P:(t + 1) * P])
                for t in range(NT):
                    for j in range(2):
                        evac(("m", t, j), hT_hi[:, 4 * j:4 * j + 4, t * P:(t + 1) * P])
                for u in range(FIRST[("w_out", 0)], NU):
                    ahead(u)
                square_x(1)
                rs_stage(6)
                for t in range(NT):
                    for j in range(2):
                        evac(("h2", t, j), h2T[:, 4 * j:4 * j + 4, t * P:(t + 1) * P])
                act.wait_ge(rt_done.sem, rt_done.at(l, 0))
                act.activation(R["score"][:].rearrange("p a b -> p (a b)"), ps[:, 4, 0:NT * N_EXP], ACT.Tanh,
                               scale=0.5).then_inc(tanh_done.sem, 1)

                def x_hi(i):
                    for j in range(2):
                        act.wait_ge(xt_done.sem, xt_done.at(l, j, i))
                        act.activation(xT_hi[:, 4 * j:4 * j + 4, :],
                                       ps[:, 5 + j, :].rearrange("p (a b) -> p a b", b=P), ACT.Copy).then_inc(xt_hi.sem, 1)

                def ys(i, first=False):
                    act.wait_ge(used[5].sem, used[5].at(l, 0, i))
                    if not first:
                        act.wait_ge(y_stored.sem, y_stored.at(l, -1, i))
                    act.activation(ysb[:, 0:512], ps[:, 2, :], ACT.Copy).then_inc(y_act.sem, 1)

                def tile(i, first=False, second=False, last=False):
                    split_hi(2, 0, i)
                    split_hi(3, 0, i)
                    if not first:
                        split_hi(4, 0, i - 1)
                        split_hi(5, 0, i - 1)
                    act.wait_ge(used[3].sem, used[3].at(l, 0, i))
                    act.activation(silu_g[:], ps[:, 0, 0:D_EXP], ACT.Silu).then_inc(silu_done.sem, 1)
                    if not last:
                        x_hi(i + 1)
                        split_hi(0, 0, i + 1)
                        split_hi(1, 0, i + 1)
                    if not first:
                        ys(i - 1, second)
                    act.wait_ge(ht_done.sem, ht_done.at(l, 0, i))
                    act.activation(hidT_hi[:], ps[:, 7, 0:2 * P].rearrange("p (a b) -> p a b", b=P),
                                   ACT.Copy).then_inc(ht_hi.sem, 1)

                x_hi(0)
                split_hi(0, 0, 0)
                split_hi(1, 0, 0)
                tile(0, first=True)
                tile(1, second=True)
                with act.Fori(2, MOE_TILES - 1) as i:
                    tile(i)
                tile(MOE_TILES - 1, last=True)
                split_hi(4, 0, MOE_TILES - 1)
                split_hi(5, 0, MOE_TILES - 1)
                ys(MOE_TILES - 1)

        @blk.vector
        def _(dve):
            dve.memset(tok_zero[:], 0).then_inc(s_zero, 1)
            dve.memset(ones_b[:], 1.0)
            dve.memset(rs_v[:], 1.0)
            dve.wait_ge(s_const, 160)
            dve.tensor_copy(tri[:], tri_f[:]).then_inc(s_tri, 1)
            dve.tensor_copy(tok_id[:], tok_id_f[:])
            dve.wait_ge(s_x, 16)
            for t in range(NT):
                dve.memset(dummy[:, t:t + 1], 0.0).then_inc(x_ready.sem, 1)
            with dve.Fori(0, DEPTH) as l:
                steps = count()

                def step():
                    return next(steps)

                def split_lo(s, n, i=None):
                    dve.wait_ge(is_hi[s].sem, is_hi[s].at(l, n, i))
                    dve.tensor_tensor(lo[s][:], raw[s][:], hi[s][:].bitcast(F32), ALU.subtract).then_inc(is_lo[s].sem, 1)

                def ahead(u):
                    w = u + LOOK
                    if w < NU and IS_SPLIT[w]:
                        split_lo(uslot[w], SPLIT_NO[w])

                def rs_stage(k, src, n, scale):
                    dve.tensor_scalar(rs_v[:, 0:n], src, scale, EPS, ALU.mult, ALU.add).then_inc(rs_in.sem, 1)
                    dve.wait_ge(rs_in.sem, rs_in.at(l, k))
                    dve.wait_ge(rs_out.sem, rs_out.at(l, k))
                    dve.tensor_tensor(rs_t[:, 0:n], rs_0[:, 0:n], rs_0[:, 0:n], ALU.mult).then_inc(dve_chain.sem, 1)
                    dve.wait_ge(dve_chain.sem, dve_chain.at(l, step()))
                    dve.tensor_tensor(rs_t[:, 0:n], rs_t[:, 0:n], rs_v[:, 0:n], ALU.mult).then_inc(dve_chain.sem, 1)
                    dve.wait_ge(dve_chain.sem, dve_chain.at(l, step()))
                    dve.tensor_scalar(rs_t[:, 0:n], rs_t[:, 0:n], -0.5, 1.5, ALU.mult, ALU.add).then_inc(dve_chain.sem, 1)
                    dve.wait_ge(dve_chain.sem, dve_chain.at(l, step()))
                    dve.tensor_tensor(rs[:, 0:n], rs_t[:, 0:n], rs_0[:, 0:n], ALU.mult).then_inc(dve_chain.sem, 1)
                    dve.wait_ge(dve_chain.sem, dve_chain.at(l, step()))

                def lo_evac(key, dst_hi, dst_lo):
                    n = TR_NO[key]
                    dve.wait_ge(tr_act.sem, tr_act.at(l, n))
                    src = ps[:, 5 + n % 2, :].rearrange("p (a b) -> p a b", b=P)
                    dve.tensor_tensor(dst_lo, src, dst_hi.bitcast(F32), ALU.subtract).then_inc(tr_dve.sem, 1)

                def norm_gain(k):
                    dve.wait_ge(nmod_loaded.sem, nmod_loaded.at(l, 3 * k + 2))
                    for cond in range(2):
                        ins = dve.scalar_tensor_tensor(out=G[:, cond, :], in0=G[:, cond, :], scalar=1.0, in1=gn[:],
                                                       op0=ALU.add, op1=ALU.mult)
                    ins.then_inc(dve_chain.sem, 1)
                    dve.wait_ge(dve_chain.sem, dve_chain.at(l, step()))
                    for t in range(NT):
                        ins = dve.tensor_tensor(hrow[:, t, :], x[:, t, :], G[:, GI(t), :], ALU.mult)
                    ins.then_inc(dve_chain.sem, 1)
                    dve.wait_ge(dve_chain.sem, dve_chain.at(l, step()))

                def norm_shift(k):
                    dve.wait_ge(shift_loaded.sem, shift_loaded.at(l, 2 * k + 1))
                    for t in range(NT):
                        dve.scalar_tensor_tensor(out=hrow[:, t, :], in0=hrow[:, t, :], scalar=rs[:, t:t + 1],
                                                 in1=sh[:, GI(t), :], op0=ALU.mult, op1=ALU.add).then_inc(h_ready.sem, 1)

                def modrow_evac(c):
                    dve.wait_ge(used[(FIRST[("mod", c)] + 3) % SLOTS].sem, used[(FIRST[("mod", c)] + 3) % SLOTS].at(l, (FIRST[("mod", c)] + 3) // SLOTS))
                    if c >= 4:
                        dve.wait_ge(mod_stored.sem, mod_stored.at(l, 4 * (c // 4) - 1))
                    dve.tensor_copy(modrow[:, c % 4, :], ps[0:2, 7, :]).then_inc(modrow_ready.sem, 1)

                dve.wait_ge(par_loaded.sem, par_loaded.at(l, 0))
                for j in range(2):
                    q0, k0 = PAR["lam_q1"][0] + 64 * j, PAR["lam_k1"][0] + 64 * j
                    ins = dve.tensor_tensor_reduce(
                        out=lam_p[:, 64 * j:64 * j + 64], in0=par[:, q0:q0 + 64], in1=par[:, k0:k0 + 64], scale=1.0,
                        scalar=0.0, op0=ALU.mult, op1=ALU.add, accum_out=lam_s[:, j:j + 1])
                ins.then_inc(lam_sum.sem, 1)
                for n in ("gq_da", "gq_na"):
                    a, b = PAR[n]
                    dve.tensor_scalar(par[:, a:b], par[:, a:b], HD ** -0.5, None, ALU.mult).then_inc(dve_chain.sem, 1)
                    dve.wait_ge(dve_chain.sem, dve_chain.at(l, step()))
                norm_gain(0)
                dve.wait_ge(xsq_done.sem, xsq_done.at(l, NT - 1))
                rs_stage(0, ssum[:, 0:NT], NT, 1.0 / D)
                a, b = PAR["g_subln"]
                c0 = PAR["one_less"][0]
                dve.tensor_scalar(gsub_s[:], par[:, a:b], par[:, c0:c0 + 1], None, ALU.mult).then_inc(dve_chain.sem, 1)
                dve.wait_ge(dve_chain.sem, dve_chain.at(l, step()))
                dve.wait_ge(lam_exp.sem, lam_exp.at(l, 0))
                c0 = PAR["lam_init"][0]
                dve.tensor_tensor(neg_lam[:], lam_e[:, 1:2], lam_e[:, 0:1], ALU.subtract).then_inc(dve_chain.sem, 1)
                dve.wait_ge(dve_chain.sem, dve_chain.at(l, step()))
                dve.tensor_tensor(neg_lam[:], neg_lam[:], par[:, c0:c0 + 1], ALU.subtract).then_inc(dve_chain.sem, 1)
                dve.wait_ge(dve_chain.sem, dve_chain.at(l, step()))
                norm_shift(0)
                for u in range(16):
                    ahead(u)
                for t in range(NT):
                    for j in range(2):
                        cs = slice(4 * j, 4 * j + 4), slice(t * P, (t + 1) * P)
                        lo_evac(("h", t, j), hT_hi[:, cs[0], cs[1]], hT_lo[:, cs[0], cs[1]])

                def head_norm(b, t, g, rotate):
                    row = stg[:, b, t, :]
                    r3 = row.rearrange("p (h d) -> p h d", d=HD)
                    dve.tensor_tensor(r3, r3, rs[:, 8 * t:8 * t + 8].unsqueeze(2).to_broadcast([P, 8, HD]),
                                      ALU.mult).then_inc(dve_chain.sem, 1)
                    dve.wait_ge(dve_chain.sem, dve_chain.at(l, step()))
                    if not (rotate and t >= 1):
                        dve.tensor_tensor(r3, r3, gain(g), ALU.mult).then_inc(qk_ready.sem, 1)
                        return
                    dve.tensor_tensor(r3, r3, gain(g), ALU.mult).then_inc(dve_chain.sem, 1)
                    dve.wait_ge(dve_chain.sem, dve_chain.at(l, step()))
                    dve.tensor_tensor(rt1[:].rearrange("p (h d) -> p h d", d=HD), r3,
                                      rope_c[:, t - 1, :].unsqueeze(1).to_broadcast([P, 8, HD]), ALU.mult)
                    r5 = row.rearrange("p (h a f n) -> p h a f n", a=2, f=2, n=16)
                    o5 = rt2[:].rearrange("p (h a f n) -> p h a f n", a=2, f=2, n=16)
                    s4 = rope_s[:, t - 1, :].rearrange("p (a f n) -> p a f n", a=2, f=2)
                    for f in range(2):
                        ins = dve.tensor_tensor(o5[:, :, :, f, :], r5[:, :, :, 1 - f, :],
                                                s4[:, :, f, :].unsqueeze(1).to_broadcast([P, 8, 2, 16]), ALU.mult)
                    ins.then_inc(dve_chain.sem, 1)
                    dve.wait_ge(dve_chain.sem, dve_chain.at(l, step()))
                    dve.tensor_tensor(row, rt1[:], rt2[:], ALU.add).then_inc(qk_ready.sem, 1)

                def qkv(first, names, rs_k, rotate):
                    for b in range(2):
                        u0 = FIRST[("w_in", first + b)]
                        if b == 0:
                            for u in range(u0, u0 + 4):
                                ahead(u)
                        for t in range(NT):
                            dve.wait_ge(pj_act.sem, pj_act.at(l, (first + b) * NT + t))
                            dve.tensor_reduce(ssum[:, 8 * t:8 * t + 8],
                                              sq[:, t % 2, :].rearrange("p (h d) -> p h d", d=HD),
                                              AX.X, ALU.add).then_inc(sum_ready.sem, 1)
                        dve.wait_ge(sum_ready.sem, sum_ready.at(l, (first // 3 * 2 + b) * NT + NT - 1))
                        rs_stage(rs_k + b, ssum[:, 0:40], 40, 1.0 / HD)
                        for t in range(NT):
                            if t < 4:
                                ahead(u0 + 4 + t)
                            head_norm(b, t, names[b], rotate)

                qkv(0, ("gq_da", "gk_da"), 1, True)
                for i in range(len(DA_UNITS) + 1):
                    if 4 <= i < 20:
                        ahead(FIRST[("mod", 4)] + i - 4)
                    if i >= 1:
                        j = i - 1
                        t, h = DA_UNITS[j]
                        nk = P if t == 0 else 640
                        b = j % 2
                        dve.wait_ge(ex_done.sem, ex_done.at(l, 2 * j + 1))
                        dve.reciprocal(rz[:, 2 * b:2 * b + 2], z[:, 2 * b:2 * b + 2]).then_inc(dve_chain.sem, 1)
                        dve.wait_ge(dve_chain.sem, dve_chain.at(l, step()))
                        dve.tensor_tensor(rz[:, 2 * b + 1:2 * b + 2], rz[:, 2 * b + 1:2 * b + 2], neg_lam[:],
                                          ALU.mult).then_inc(dve_chain.sem, 1)
                        dve.wait_ge(dve_chain.sem, dve_chain.at(l, step()))
                        dve.tensor_scalar(e_da[:, b, 1, 0:nk], e_da[:, b, 1, 0:nk],
                                          rz[:, 2 * b + 1:2 * b + 2], None, ALU.mult).then_inc(dve_chain.sem, 1)
                        dve.wait_ge(dve_chain.sem, dve_chain.at(l, step()))
                        if j >= 2:
                            tj = DA_UNITS[j - 2][0]
                            dve.wait_ge(tr_done.sem, tr_done.at(l, TR_NO[("p", j - 2, 1 if tj else 0)]))
                        dve.scalar_tensor_tensor(out=a_da[:, b, 0:nk], in0=e_da[:, b, 0, 0:nk],
                                                 scalar=rz[:, 2 * b:2 * b + 1], in1=e_da[:, b, 1, 0:nk],
                                                 op0=ALU.mult, op1=ALU.add).then_inc(cb_done.sem, 1)
                    if i < len(DA_UNITS):
                        nk = P if DA_UNITS[i][0] == 0 else 640
                        for m in range(2):
                            dve.wait_ge(sc_done.sem, sc_done.at(l, 2 * i + m))
                            c = 2 * (i % 2) + m
                            dve.tensor_reduce(neg_m[:, c:c + 1], ps_flat[:, m * 1024:m * 1024 + nk],
                                              AX.X, ALU.max, negate=True).then_inc(mx_done.sem, 1)
                    if i >= 1:
                        if h == DA_HEADS - 1:
                            dve.wait_ge(oc_done.sem, oc_done.at(l, t))
                            dve.tensor_reduce(o_ssum[:, 4 * t:4 * t + 4],
                                              sq[:, 0, :].rearrange("p (h d) -> p h d", d=P), AX.X, ALU.add).then_inc(oss_done.sem, 1)
                    if i % 4 == 0 and i >= 8:
                        modrow_evac(2 + i // 4)
                dve.wait_ge(oss_done.sem, oss_done.at(l, NT - 1))
                rs_stage(3, o_ssum[:], 20, 1.0 / P)
                for t in range(NT):
                    o3 = o_a[:, t, :].rearrange("p (h d) -> p h d", d=P)
                    dve.tensor_tensor(o3, o3, rs[:, 4 * t:4 * t + 4].unsqueeze(2).to_broadcast([P, 4, P]),
                                      ALU.mult).then_inc(dve_chain.sem, 1)
                    dve.wait_ge(dve_chain.sem, dve_chain.at(l, step()))
                    dve.tensor_tensor(o3, o3, gsub_s[:].unsqueeze(1).to_broadcast([P, 4, P]), ALU.mult).then_inc(oa_ready.sem, 1)
                qkv(3, ("gq_na", "gk_na"), 4, False)
                for i in range(len(NA_UNITS) + 2):
                    if i % 2 == 0 and i < 32:
                        ahead(FIRST[("mod", 8)] + i // 2)
                    if i < len(NA_UNITS):
                        t, h = NA_UNITS[i]
                        dve.wait_ge(nsc_done.sem, nsc_done.at(l, i))
                        if i >= 2:
                            dve.wait_ge(nex_done.sem, nex_done.at(l, i - 2))
                        if t == 0:
                            dve.tensor_reduce(neg_m[:, i % 2:i % 2 + 1], ps[:, i % 4, 0:P], AX.X, ALU.max,
                                              negate=True).then_inc(nmx_done.sem, 1)
                        else:
                            j = (i - NA_HEADS) // 2
                            if h % 2 == 0:
                                dve.wait_ge(bias_ld[j % 2].sem, bias_ld[j % 2].at(l, j // 2))
                            dve.sem_inc(s_settled, 1)
                            dve.tensor_tensor_reduce(out=s_na[:, i % 2, :], in0=ps[:, i % 4, 0:WKEYS],
                                                     in1=bias_na[:, j % 2, h % 2, :], scale=1.0, scalar=-3.0e38,
                                                     op0=ALU.add, op1=ALU.max, accum_out=rs_t[:, 0:1]).then_inc(dve_chain.sem, 1)
                            dve.wait_ge(dve_chain.sem, dve_chain.at(l, step()))
                            dve.tensor_scalar(neg_m[:, i % 2:i % 2 + 1], rs_t[:, 0:1], -1.0, None, ALU.mult).then_inc(nmx_done.sem, 1)
                    if 1 <= i <= len(NA_UNITS):
                        j = i - 1
                        t, h = NA_UNITS[j]
                        nk = P if t == 0 else WKEYS
                        dve.wait_ge(nex_done.sem, nex_done.at(l, j))
                        dve.reciprocal(rz[:, j % 2:j % 2 + 1], z[:, j % 2:j % 2 + 1]).then_inc(dve_chain.sem, 1)
                        dve.wait_ge(dve_chain.sem, dve_chain.at(l, step()))
                        if j >= 2:
                            dve.wait_ge(tr_done.sem, tr_done.at(l, TR_NO[("np", j - 2)]))
                        dve.tensor_scalar(p_na[:, j % 2, 0:nk], e_na[:, j % 2, 0:nk], rz[:, j % 2:j % 2 + 1],
                                          None, ALU.mult).then_inc(np_done.sem, 1)
                    if i >= 2:
                        t, h = NA_UNITS[i - 2]
                        if h == NA_HEADS - 1:
                            if t == 0:
                                dve.wait_ge(kv_out.sem, kv_out.at(l, 3))
                            dve.wait_ge(nob_hi.sem, nob_hi.at(l, t))
                            cs = slice(t * P, (t + 1) * P)
                            dve.tensor_tensor(oTb_lo[:, :, cs],
                                              ps[:, 4, :].rearrange("p (a b) -> p a b", b=P),
                                              oTb_hi[:, :, cs].bitcast(F32), ALU.subtract).then_inc(nob_done.sem, 1)
                    if i % 8 == 7 and i < 32:
                        modrow_evac(8 + i // 8)
                for c in range(2):
                    for which, kind in enumerate((("w_in", 6 + c), ("br_a", c), ("w_in", 8 + c), ("br_b", c))):
                        for u in range(FIRST[kind], FIRST[kind] + KQ[kind[0]]):
                            ahead(u)
                        if c == 0 and which == 0:
                            for t in range(NT):
                                cs = slice(t * P, (t + 1) * P)
                                lo_evac(("o", t), oTa_hi[:, :, cs], oTa_lo[:, :, cs])
                        if kind[0] == "w_in":
                            continue
                        for t in range(NT):
                            dve.wait_ge(*sums(l, kind, t))
                            dve.wait_ge(pj_act.sem, pj_act.at(l, PJ_ACT.index(("w_in", (6 if which == 1 else 8) + c)) * NT + t))
                            dst = mixed[:, t, c * 512:(c + 1) * 512]
                            if which == 1:
                                dve.tensor_tensor(dst, ps[:, t, :], sg[:, t, :], ALU.mult).then_inc(pj_dve.sem, 1)
                            else:
                                dve.tensor_tensor(tmp[:, t % 2, :], ps[:, t, :], sg[:, t, :], ALU.mult).then_inc(pj_dve.sem, 1)
                                dve.wait_ge(pj_dve.sem, pj_dve.at(l, PJ_DVE.index(kind) * NT + t))
                                ins = dve.tensor_tensor(dst, dst, tmp[:, t % 2, :], ALU.add)
                                if c == 1:
                                    ins.then_inc(mixed_ready.sem, 1)
                                else:
                                    ins.then_inc(dve_chain.sem, 1)
                                    step()
                for t in range(NT):
                    for j in range(2):
                        cs = slice(4 * j, 4 * j + 4), slice(t * P, (t + 1) * P)
                        lo_evac(("m", t, j), hT_hi[:, cs[0], cs[1]], hT_lo[:, cs[0], cs[1]])
                dve.wait_ge(x_back.sem, x_back.at(l, 0))
                dve.wait_ge(gate_loaded.sem, gate_loaded.at(l, 1))
                for c in range(2):
                    kind = ("w_out", c)
                    for u in range(FIRST[kind], FIRST[kind] + 4):
                        ahead(u)
                    for t in range(NT):
                        dve.wait_ge(*sums(l, kind, t))
                        cs = slice(c * 512, (c + 1) * 512)
                        dve.tensor_tensor(tmp[:, t % 2, :], ps[:, t, :], gt[:, GI(t), cs], ALU.mult).then_inc(pj_dve.sem, 1)
                        dve.wait_ge(pj_dve.sem, pj_dve.at(l, PJ_DVE.index(kind) * NT + t))
                        ins = dve.tensor_tensor(x[:, t, cs], x[:, t, cs], tmp[:, t % 2, :], ALU.add)
                        if c == 1:
                            ins.then_inc(xu_done.sem, 1)
                        else:
                            ins.then_inc(dve_chain.sem, 1)
                            dve.wait_ge(dve_chain.sem, dve_chain.at(l, step()))
                norm_gain(1)
                dve.wait_ge(xsq_done.sem, xsq_done.at(l, 2 * NT - 1))
                rs_stage(6, ssum[:, 0:NT], NT, 1.0 / D)
                norm_shift(1)
                dve.wait_ge(tanh_done.sem, tanh_done.at(l, 0))
                flat = lambda a: a[:].rearrange("p a b -> p (a b)")
                TT, TS, STT = dve.tensor_tensor, dve.tensor_scalar, dve.scalar_tensor_tensor
                bc_e = lambda a: a.unsqueeze(2).to_broadcast([P, NT, N_EXP])
                bc_t = lambda a: a.unsqueeze(1).to_broadcast([P, NT, N_EXP])
                score, sel, cand, oh1, oh2, selm, slot = (R[n][:] for n in
                                                          ("score", "sel", "cand", "oh1", "oh2", "selm", "slot"))
                TS(score, score, 0.5, 0.5, ALU.mult, ALU.add).then_inc(dve_chain.sem, 1)
                dve.wait_ge(dve_chain.sem, dve_chain.at(l, step()))
                TT(sel, score, bc_t(br_b[:]), ALU.add).then_inc(dve_chain.sem, 1)
                dve.wait_ge(dve_chain.sem, dve_chain.at(l, step()))
                s5 = sel.rearrange("p t (g k c) -> p t g k c", g=N_GRP, k=2)
                M = {n: r_m[n][:] for n in r_m}
                TT(M["hi"], s5[:, :, :, 0, 0], s5[:, :, :, 0, 1], ALU.max).then_inc(dve_chain.sem, 1)
                dve.wait_ge(dve_chain.sem, dve_chain.at(l, step()))
                TT(M["lo"], s5[:, :, :, 0, 0], s5[:, :, :, 0, 1], ALU.min).then_inc(dve_chain.sem, 1)
                dve.wait_ge(dve_chain.sem, dve_chain.at(l, step()))
                TT(M["hi2"], s5[:, :, :, 1, 0], s5[:, :, :, 1, 1], ALU.max).then_inc(dve_chain.sem, 1)
                dve.wait_ge(dve_chain.sem, dve_chain.at(l, step()))
                TT(M["a"], s5[:, :, :, 1, 0], s5[:, :, :, 1, 1], ALU.min).then_inc(dve_chain.sem, 1)
                dve.wait_ge(dve_chain.sem, dve_chain.at(l, step()))
                TT(M["lo"], M["lo"], M["a"], ALU.max).then_inc(dve_chain.sem, 1)
                dve.wait_ge(dve_chain.sem, dve_chain.at(l, step()))
                TT(M["a"], M["hi"], M["hi2"], ALU.min).then_inc(dve_chain.sem, 1)
                dve.wait_ge(dve_chain.sem, dve_chain.at(l, step()))
                TT(M["lo"], M["lo"], M["a"], ALU.max).then_inc(dve_chain.sem, 1)
                dve.wait_ge(dve_chain.sem, dve_chain.at(l, step()))
                TT(M["hi"], M["hi"], M["hi2"], ALU.max).then_inc(dve_chain.sem, 1)
                dve.wait_ge(dve_chain.sem, dve_chain.at(l, step()))
                TT(M["gs"], M["hi"], M["lo"], ALU.add).then_inc(dve_chain.sem, 1)
                dve.wait_ge(dve_chain.sem, dve_chain.at(l, step()))

                def first_max(src, n, mx, cnd, out):
                    bc = lambda a: a.unsqueeze(2).to_broadcast([P, NT, n])
                    io = iota_e[:, 0:n].unsqueeze(1).to_broadcast([P, NT, n])
                    dve.tensor_reduce(mx, src, AX.X, ALU.max).then_inc(dve_chain.sem, 1)
                    dve.wait_ge(dve_chain.sem, dve_chain.at(l, step()))
                    TT(cnd, src, bc(mx), ALU.is_equal).then_inc(dve_chain.sem, 1)
                    dve.wait_ge(dve_chain.sem, dve_chain.at(l, step()))
                    STT(out=cnd, in0=cnd, scalar=-100.0, in1=io, op0=ALU.mult, op1=ALU.add).then_inc(dve_chain.sem, 1)
                    dve.wait_ge(dve_chain.sem, dve_chain.at(l, step()))
                    dve.tensor_reduce(mx, cnd, AX.X, ALU.min).then_inc(dve_chain.sem, 1)
                    dve.wait_ge(dve_chain.sem, dve_chain.at(l, step()))
                    TT(out, cnd, bc(mx), ALU.is_equal).then_inc(dve_chain.sem, 1)
                    dve.wait_ge(dve_chain.sem, dve_chain.at(l, step()))

                m1 = r_1["m"][:]
                first_max(M["gs"], 4, m1, M["gc"], M["goh"])
                in_g = M["goh"].unsqueeze(3).to_broadcast([P, NT, N_GRP, 4])
                g4 = lambda a: a.rearrange("p t (g k) -> p t g k", g=N_GRP)
                TS(M["gc"], M["goh"], -NEG, NEG, ALU.mult, ALU.add).then_inc(dve_chain.sem, 1)
                dve.wait_ge(dve_chain.sem, dve_chain.at(l, step()))
                TT(g4(selm), g4(sel), in_g, ALU.mult).then_inc(dve_chain.sem, 1)
                dve.wait_ge(dve_chain.sem, dve_chain.at(l, step()))
                TT(g4(selm), g4(selm), M["gc"].unsqueeze(3).to_broadcast([P, NT, N_GRP, 4]), ALU.add).then_inc(dve_chain.sem, 1)
                dve.wait_ge(dve_chain.sem, dve_chain.at(l, step()))
                first_max(selm, N_EXP, m1, cand, oh1)
                STT(out=selm, in0=oh1, scalar=4.0 * NEG, in1=selm, op0=ALU.mult, op1=ALU.add).then_inc(dve_chain.sem, 1)
                dve.wait_ge(dve_chain.sem, dve_chain.at(l, step()))
                first_max(selm, N_EXP, m1, cand, oh2)
                TT(member[:], oh1, oh2, ALU.add).then_inc(member_ready.sem, 1)
                for n, oh in (("s1", oh1), ("s2", oh2)):
                    TT(cand, score, oh, ALU.mult).then_inc(dve_chain.sem, 1)
                    dve.wait_ge(dve_chain.sem, dve_chain.at(l, step()))
                    dve.tensor_reduce(r_1[n][:], cand, AX.X, ALU.add).then_inc(dve_chain.sem, 1)
                    dve.wait_ge(dve_chain.sem, dve_chain.at(l, step()))
                TT(m1, r_1["s1"][:], r_1["s2"][:], ALU.add).then_inc(dve_chain.sem, 1)
                dve.wait_ge(dve_chain.sem, dve_chain.at(l, step()))
                dve.reciprocal(m1, m1).then_inc(dve_chain.sem, 1)
                dve.wait_ge(dve_chain.sem, dve_chain.at(l, step()))
                TT(r_1["w1"][:], r_1["s1"][:], m1, ALU.mult).then_inc(dve_chain.sem, 1)
                dve.wait_ge(dve_chain.sem, dve_chain.at(l, step()))
                TT(r_1["w2"][:], r_1["s2"][:], m1, ALU.mult).then_inc(dve_chain.sem, 1)
                dve.wait_ge(dve_chain.sem, dve_chain.at(l, step()))
                dve.wait_ge(pos_done.sem, pos_done.at(l, 0))
                rank = ps[:, 3, 0:NT * N_EXP].rearrange("p (a b) -> p a b", b=N_EXP)
                total = ps[:, 3, NT * N_EXP:(NT + 1) * N_EXP]
                TS(n_tiles[:], total, 0.0, None, ALU.is_gt).then_inc(dve_chain.sem, 1)
                dve.wait_ge(dve_chain.sem, dve_chain.at(l, step()))
                for k in range(1, NT):
                    STT(out=n_tiles[:], in0=total, scalar=float(k * P), in1=n_tiles[:], op0=ALU.is_gt,
                        op1=ALU.add).then_inc(dve_chain.sem, 1)
                    dve.wait_ge(dve_chain.sem, dve_chain.at(l, step()))
                TS(end_t[:], n_tiles[:], 1.0, None, ALU.mult).then_inc(dve_chain.sem, 1)
                dve.wait_ge(dve_chain.sem, dve_chain.at(l, step()))
                for k in (1, 2, 4, 8):
                    TS(base_s[:], end_t[:], 1.0, None, ALU.mult).then_inc(dve_chain.sem, 1)
                    dve.wait_ge(dve_chain.sem, dve_chain.at(l, step()))
                    TT(end_t[:, k:], base_s[:, k:], base_s[:, 0:N_EXP - k], ALU.add).then_inc(dve_chain.sem, 1)
                    dve.wait_ge(dve_chain.sem, dve_chain.at(l, step()))
                TT(base_s[:], end_t[:], n_tiles[:], ALU.subtract).then_inc(dve_chain.sem, 1)
                dve.wait_ge(dve_chain.sem, dve_chain.at(l, step()))
                STT(out=slot, in0=bc_t(base_s[:]), scalar=float(P), in1=rank, op0=ALU.mult, op1=ALU.add).then_inc(dve_chain.sem, 1)
                dve.wait_ge(dve_chain.sem, dve_chain.at(l, step()))
                for j, oh in enumerate((oh1, oh2)):
                    TT(cand, slot, oh, ALU.mult).then_inc(dve_chain.sem, 1)
                    dve.wait_ge(dve_chain.sem, dve_chain.at(l, step()))
                    dve.tensor_reduce(slot_f[:, j, :], cand, AX.X, ALU.add).then_inc(dve_chain.sem, 1)
                    dve.wait_ge(dve_chain.sem, dve_chain.at(l, step()))
                dve.tensor_copy(slot_i[:], slot_f[:]).then_inc(slot_ready.sem, 1)
                TT(ecmp[:], iota_t[:].unsqueeze(2).to_broadcast([P, MOE_TILES, N_EXP]),
                   end_t[:].unsqueeze(1).to_broadcast([P, MOE_TILES, N_EXP]), ALU.is_ge).then_inc(dve_chain.sem, 1)
                dve.wait_ge(dve_chain.sem, dve_chain.at(l, step()))
                dve.tensor_reduce(etab_f[:], ecmp[:], AX.X, ALU.add).then_inc(dve_chain.sem, 1)
                dve.wait_ge(dve_chain.sem, dve_chain.at(l, step()))
                TS(etab[:], etab_f[:], float(N_EXP - 1), None, ALU.min).then_inc(etab_ready.sem, 1)

                def x_lo(i):
                    for j in range(2):
                        dve.wait_ge(xt_hi.sem, xt_hi.at(l, j, i))
                        dve.tensor_tensor(xT_lo[:, 4 * j:4 * j + 4, :],
                                          ps[:, 5 + j, :].rearrange("p (a b) -> p a b", b=P),
                                          xT_hi[:, 4 * j:4 * j + 4, :].bitcast(F32), ALU.subtract).then_inc(xt_lo.sem, 1)

                def ys(i, first=False):
                    dve.wait_ge(used[5].sem, used[5].at(l, 0, i))
                    if not first:
                        dve.wait_ge(y_stored.sem, y_stored.at(l, -1, i))
                    dve.tensor_copy(ysb[:, 512:1024], ps[:, 3, :]).then_inc(y_dve.sem, 1)

                def tile(i, first=False, second=False, last=False):
                    split_lo(2, 0, i)
                    split_lo(3, 0, i)
                    if not first:
                        split_lo(4, 0, i - 1)
                        split_lo(5, 0, i - 1)
                    dve.wait_ge(silu_done.sem, silu_done.at(l, 0, i))
                    dve.tensor_tensor(hid[:], ps[:, 0, D_EXP:2 * D_EXP], silu_g[:], ALU.mult).then_inc(hid_done.sem, 1)
                    if not last:
                        x_lo(i + 1)
                        split_lo(0, 0, i + 1)
                        split_lo(1, 0, i + 1)
                    if not first:
                        ys(i - 1, second)
                    dve.wait_ge(ht_hi.sem, ht_hi.at(l, 0, i))
                    dve.tensor_tensor(hidT_lo[:], ps[:, 7, 0:2 * P].rearrange("p (a b) -> p a b", b=P),
                                      hidT_hi[:].bitcast(F32), ALU.subtract).then_inc(ht_lo.sem, 1)

                x_lo(0)
                split_lo(0, 0, 0)
                split_lo(1, 0, 0)
                tile(0, first=True)
                tile(1, second=True)
                with dve.Fori(2, MOE_TILES - 1) as i:
                    tile(i)
                tile(MOE_TILES - 1, last=True)
                split_lo(4, 0, MOE_TILES - 1)
                split_lo(5, 0, MOE_TILES - 1)
                ys(MOE_TILES - 1)
                dve.wait_ge(gate_loaded.sem, gate_loaded.at(l, 3))
                for t in range(NT):
                    dve.wait_ge(gathered[t % 2].sem, gathered[t % 2].at(l, 2 * (t // 2) + 1))
                    y1, y2 = yg[:, t % 2, 0, :], yg[:, t % 2, 1, :]
                    TS(y1, y1, r_1["w1"][:, t:t + 1], None, ALU.mult).then_inc(dve_chain.sem, 1)
                    dve.wait_ge(dve_chain.sem, dve_chain.at(l, step()))
                    STT(out=y1, in0=y2, scalar=r_1["w2"][:, t:t + 1], in1=y1, op0=ALU.mult, op1=ALU.add).then_inc(dve_chain.sem, 1)
                    dve.wait_ge(dve_chain.sem, dve_chain.at(l, step()))
                    TT(y1, y1, gt[:, GI(t), :], ALU.mult).then_inc(dve_chain.sem, 1)
                    dve.wait_ge(dve_chain.sem, dve_chain.at(l, step()))
                    TT(x[:, t, :], x[:, t, :], y1, ALU.add).then_inc(x_ready.sem, 1)
                n = step()
                assert n == DVE_CHAIN, n

        @blk.tensor
        def _(pe):
            pe.wait_ge(s_const, 160)
            pe.wait_ge(s_cact, 1)
            pe.wait_ge(s_tri, 1)
            with pe.Fori(0, DEPTH) as l:

                def mod_unit(u):
                    _, c, k = UNITS[u]
                    s = uslot[u]
                    if k == 0 and c >= 5:
                        pe.wait_ge(modrow_ready.sem, modrow_ready.at(l, c - 1))
                    pe.wait_ge(loaded[s].sem, loaded[s].at(l, u // SLOTS))
                    for j in range(2):
                        ins = pe.matmul(ps[0:2, MOD_BANK[c], :], c_act[:, 2 * k + j, :], raw[s][:, j, :],
                                        start=(k == 0 and j == 0), stop=(k == 3 and j == 1))
                    ins.then_inc(used[s].sem, 1)

                def transposes(key, srcs):
                    n = TR_NO[key]
                    if n >= 2:
                        before, split = TR[n - 2]
                        if split:
                            pe.wait_ge(tr_dve.sem, tr_dve.at(l, TR_SPLIT_NO[before]))
                        else:
                            pe.wait_ge(tr_act.sem, tr_act.at(l, n - 2))
                    for j, src in enumerate(srcs):
                        ins = pe.transpose(ps[:, 5 + n % 2, j * P:(j + 1) * P], src, ident[:])
                    ins.then_inc(tr_done.sem, 1)

                def blocks(ap, n=4):
                    return [ap[:, j * P:(j + 1) * P] for j in range(n)]

                def pass3(out, w_hi, w_lo, m_hi, m_lo, first, last):
                    pe.matmul(out, w_hi, m_hi, start=first, stop=False)
                    pe.matmul(out, w_hi, m_lo, start=False, stop=False)
                    return pe.matmul(out, w_lo, m_hi, start=False, stop=last)

                def project(kind, src_hi, src_lo):
                    b = PJ.index(kind)
                    nq = KQ[kind[0]]
                    for k in range(nq):
                        u = FIRST[kind] + k
                        s = uslot[u]
                        pe.wait_ge(is_lo[s].sem, is_lo[s].at(l, SPLIT_NO[u]))
                        for t in range(NT):
                            if k == 0 and b > 0:
                                pb = PJ[b - 1]
                                if pb in PJ_ACT:
                                    pe.wait_ge(pj_act.sem, pj_act.at(l, PJ_ACT.index(pb) * NT + t))
                                else:
                                    pe.wait_ge(pj_dve.sem, pj_dve.at(l, PJ_DVE.index(pb) * NT + t))
                            cs = slice(t * P, (t + 1) * P)
                            for j in range(2):
                                kc = 2 * k + j
                                ins = pass3(ps[:, t, :], src_hi[:, kc, cs], src_lo[:, kc, cs], hi[s][:, j, :],
                                            lo[s][:, j, :], kc == 0, kc == 2 * nq - 1)
                            if k == nq - 1 and t < NT - 1:
                                ins.then_inc(pj_done.sem, 1)
                        ins.then_inc(used[s].sem, 1)

                for u in range(16):
                    mod_unit(u)
                for t in range(NT):
                    pe.wait_ge(h_ready.sem, h_ready.at(l, t))
                    for j in range(2):
                        transposes(("h", t, j), blocks(hrow[:, t, 512 * j:512 * j + 512]))
                pe.wait_ge(tr_dve.sem, tr_dve.at(l, TR_SPLIT_NO[("h", NT - 1, 1)]))

                def qkv(first, names):
                    e = first // 3 * 2
                    project(("w_in", first), hT_hi, hT_lo)
                    project(("w_in", first + 1), hT_hi, hT_lo)
                    for t in range(NT):
                        pe.wait_ge(qk_ready.sem, qk_ready.at(l, e * NT + t))
                        transposes((names[0], t), blocks(stg[:, 0, t, :]))
                    project(("w_in", first + 2), hT_hi, hT_lo)
                    for t in range(NT):
                        pe.wait_ge(qk_ready.sem, qk_ready.at(l, (e + 1) * NT + t))
                        transposes((names[1], t), blocks(stg[:, 1, t, :]))
                    pe.wait_ge(tr_act.sem, tr_act.at(l, TR_NO[(names[1], NT - 1)]))
                    pe.wait_ge(pj_act.sem, pj_act.at(l, (first + 2) * NT + NT - 1))

                qkv(0, ("q", "k"))

                def da_scores(i):
                    t, h = DA_UNITS[i]
                    if (t, h) == (1, 0):
                        pe.wait_ge(ctx_k.sem, ctx_k.at(l, 0))
                        pe.wait_ge(ctx_v.sem, ctx_v.at(l, 0))
                    po = 64 * (h % 2)
                    for m in range(2):
                        c = 2 * m + h // 2
                        q = qT[po:po + 64, c, t * P:(t + 1) * P]
                        if i >= 1:
                            pe.wait_ge(ex_done.sem, ex_done.at(l, 2 * (i - 1) + m))
                        if t == 0:
                            ins = pe.matmul(ps[:, 2 * m, 0:P], q, kT[po:po + 64, c, PROMPT:PROMPT + P],
                                            start=True, stop=True)
                        else:
                            pe.matmul(ps[:, 2 * m, :], q, kT[po:po + 64, c, 0:512], start=True, stop=True)
                            ins = pe.matmul(ps[:, 2 * m + 1, 0:P], q, kT[po:po + 64, c, CTX:CTX + P],
                                            start=True, stop=True)
                        ins.then_inc(sc_done.sem, 1)

                da_scores(0)
                for i, (t, h) in enumerate(DA_UNITS):
                    if i + 1 < len(DA_UNITS):
                        da_scores(i + 1)
                    b = i % 2
                    pe.wait_ge(cb_done.sem, cb_done.at(l, i))
                    transposes(("p", i, 0), blocks(a_da[:, b, :], 1 if t == 0 else 4))
                    if t:
                        transposes(("p", i, 1), [a_da[:, b, 512:640]])
                    if i >= 4:
                        mod_unit(FIRST[("mod", 4)] + i - 4)
                    pe.wait_ge(tr_act.sem, tr_act.at(l, TR_NO[("p", i, 1 if t else 0)]))
                    if h == 0 and t >= 1:
                        pe.wait_ge(oc_done.sem, oc_done.at(l, t - 1))
                    chunks = [5] if t == 0 else range(5)
                    for n, c in enumerate(chunks):
                        ins = pe.matmul(ps[:, 4, h * P:(h + 1) * P], pT[:, b, n, :], v[:, c, h * P:(h + 1) * P],
                                        start=(n == 0), stop=(n == len(chunks) - 1))
                    if h == DA_HEADS - 1:
                        ins.then_inc(av_done.sem, 1)
                pe.wait_ge(oc_done.sem, oc_done.at(l, NT - 1))
                qkv(3, ("nq", "nk"))

                def na_scores(i):
                    t, h = NA_UNITS[i]
                    if (t, h) == (1, 0):
                        pe.wait_ge(ctx_k.sem, ctx_k.at(l, 1))
                        pe.wait_ge(ctx_v.sem, ctx_v.at(l, 1))
                        pe.wait_ge(v_shifted.sem, v_shifted.at(l, 1))
                    po, c = 64 * (h % 2), h // 2
                    q = qT[po:po + 64, c, t * P:(t + 1) * P]
                    if i >= 4:
                        pe.wait_ge(nex_done.sem, nex_done.at(l, i - 4))
                    if t == 0:
                        ins = pe.matmul(ps[:, i % 4, 0:P], q, kT[po:po + 64, c, PROMPT:PROMPT + P],
                                        start=True, stop=True)
                    else:
                        w = WSTART[t - 1]
                        pe.matmul(ps[:, i % 4, 0:WIN], q, kT[po:po + 64, c, w:w + WIN], start=True, stop=True)
                        ins = pe.matmul(ps[:, i % 4, WIN:WKEYS], q, kT[po:po + 64, c, CTX:CTX + P],
                                        start=True, stop=True)
                    ins.then_inc(nsc_done.sem, 1)

                na_scores(0)
                na_scores(1)
                def na_values(i):
                    t, h = NA_UNITS[i]
                    b = i % 2
                    pe.wait_ge(tr_act.sem, tr_act.at(l, TR_NO[("np", i)]))
                    if h == 0 and t >= 1:
                        pe.wait_ge(nob_done.sem, nob_done.at(l, t - 1))
                    if t == 0:
                        vals = [v[:, 5, :]]
                    else:
                        w = WSTART[t - 1] // 64
                        vals = [v[:, w // 2, :], v[:, w // 2 + 1, :]] if w % 2 == 0 else \
                               [v_sh[:, w // 2, :], v_sh[:, w // 2 + 1, :]]
                        vals.append(v[:, 4, :])
                    po, c = 64 * (h % 2), h // 2
                    for n, val in enumerate(vals):
                        ins = pe.matmul(ps[po:po + 64, 4, c * P:(c + 1) * P], val[:, h * HD:(h + 1) * HD],
                                        pT_na[:, b, n, :], start=(n == 0), stop=(n == len(vals) - 1))
                    if h == NA_HEADS - 1:
                        ins.then_inc(nav_done.sem, 1)

                for i, (t, h) in enumerate(NA_UNITS):
                    if i + 2 < len(NA_UNITS):
                        na_scores(i + 2)
                    pe.wait_ge(np_done.sem, np_done.at(l, i))
                    transposes(("np", i), blocks(p_na[:, i % 2, :], 1 if t == 0 else 3))
                    if i >= 1:
                        na_values(i - 1)
                    if i % 2 == 0 and i < 32:
                        mod_unit(FIRST[("mod", 8)] + i // 2)
                na_values(len(NA_UNITS) - 1)
                pe.wait_ge(nob_done.sem, nob_done.at(l, NT - 1))
                for c in range(2):
                    project(("w_in", 6 + c), hT_hi, hT_lo)
                    if c == 0:
                        for t in range(NT):
                            pe.wait_ge(oa_ready.sem, oa_ready.at(l, t))
                            transposes(("o", t), blocks(o_a[:, t, :]))
                        pe.wait_ge(tr_dve.sem, tr_dve.at(l, TR_SPLIT_NO[("o", NT - 1)]))
                    project(("br_a", c), oTa_hi, oTa_lo)
                    project(("w_in", 8 + c), hT_hi, hT_lo)
                    project(("br_b", c), oTb_hi, oTb_lo)
                for t in range(NT):
                    pe.wait_ge(mixed_ready.sem, mixed_ready.at(l, t))
                    for j in range(2):
                        transposes(("m", t, j), blocks(mixed[:, t, 512 * j:512 * j + 512]))
                pe.wait_ge(tr_dve.sem, tr_dve.at(l, TR_SPLIT_NO[("m", NT - 1, 1)]))
                for c in range(2):
                    project(("w_out", c), hT_hi, hT_lo)
                for t in range(NT):
                    pe.wait_ge(h_ready.sem, h_ready.at(l, NT + t))
                    for j in range(2):
                        transposes(("h2", t, j), blocks(hrow[:, t, 512 * j:512 * j + 512]))
                pe.wait_ge(tr_act.sem, tr_act.at(l, TR_NO[("h2", NT - 1, 1)]))
                for t in range(NT):
                    for k in range(KC):
                        ins = pe.matmul(ps[:, 4, t * N_EXP:(t + 1) * N_EXP], h2T[:, k, t * P:(t + 1) * P], wr[:, k, :],
                                        start=(k == 0), stop=(k == KC - 1))
                ins.then_inc(rt_done.sem, 1)
                pe.wait_ge(member_ready.sem, member_ready.at(l, 0))
                for t in range(NT + 1):
                    out = ps[:, 3, t * N_EXP:(t + 1) * N_EXP]
                    for j in range(t):
                        ins = pe.matmul(out, ones_b[:], member[:, j, :], start=(j == 0), stop=(j == NT - 1))
                    if t < NT:
                        pe.matmul(out, tri[:], member[:, t, :], start=(t == 0), stop=True)
                ins.then_inc(pos_done.sem, 1)

                def x_transposes(i):
                    pe.wait_ge(xg_loaded.sem, xg_loaded.at(l, 0, i))
                    for j in range(2):
                        for n in range(4):
                            c = 4 * j + n
                            ins = pe.transpose(ps[:, 5 + j, n * P:(n + 1) * P], xg[:, c * P:(c + 1) * P], ident[:])
                        ins.then_inc(xt_done.sem, 1)

                def gate_up(i, first=False):
                    pe.wait_ge(xt_lo.sem, xt_lo.at(l, 1, i))
                    if not first:
                        pe.wait_ge(hid_done.sem, hid_done.at(l, -1, i))
                    for s in range(4):
                        pe.wait_ge(is_lo[s].sem, is_lo[s].at(l, 0, i))
                        for j in range(2):
                            kc = 2 * s + j
                            ins = pass3(ps[:, 0, :], xT_hi[:, kc, :], xT_lo[:, kc, :], hi[s][:, j, :], lo[s][:, j, :],
                                        kc == 0, kc == KC - 1)
                        ins.then_inc(used[s].sem, 1)

                def down(i, first=False):
                    pe.wait_ge(ht_lo.sem, ht_lo.at(l, 0, i))
                    if not first:
                        pe.wait_ge(y_act.sem, y_act.at(l, -1, i))
                        pe.wait_ge(y_dve.sem, y_dve.at(l, -1, i))
                    for k in range(2):
                        s = 4 + k
                        pe.wait_ge(is_lo[s].sem, is_lo[s].at(l, 0, i))
                        for n in range(2):
                            ins = pass3(ps[:, 2 + n, :], hidT_hi[:, k, :], hidT_lo[:, k, :], hi[s][:, n, :],
                                        lo[s][:, n, :], k == 0, k == 1)
                        ins.then_inc(used[s].sem, 1)

                def hid_transposes(i):
                    pe.wait_ge(hid_done.sem, hid_done.at(l, 0, i))
                    for j in range(2):
                        ins = pe.transpose(ps[:, 7, j * P:(j + 1) * P], hid[:, j * P:(j + 1) * P], ident[:])
                    ins.then_inc(ht_done.sem, 1)

                pe.wait_ge(modrow_ready.sem, modrow_ready.at(l, 11))
                x_transposes(0)
                gate_up(0, first=True)
                x_transposes(1)
                hid_transposes(0)
                gate_up(1)
                x_transposes(2)
                down(0, first=True)
                hid_transposes(1)
                with pe.Fori(2, MOE_TILES - 1) as i:
                    gate_up(i)
                    x_transposes(i + 1)
                    down(i - 1)
                    hid_transposes(i)
                gate_up(MOE_TILES - 1)
                down(MOE_TILES - 2)
                hid_transposes(MOE_TILES - 1)
                down(MOE_TILES - 1)


_RUN_INS = ("w_stream", "w_moe", "x_in", "c_cols", "params", "b_mod2", "g_norms", "da_kc", "da_vc", "na_kc", "na_vc",
            "na_bias", "w_router", "b_router", "consts", "rope")


def bias_index():
    out = np.full((4, P, WIN), -1, np.int64)
    for t in range(4):
        tok = t * P + np.arange(P)
        qc, qr = tok // ROWS, tok % ROWS
        key = WSTART[t] + np.arange(WIN)
        kc, kr = key // ROWS, key % ROWS
        c0 = np.clip(qc - 8, 0, GRID_W - 16)
        ok = (kc[None] >= c0[:, None]) & (kc[None] < c0[:, None] + 16)
        idx = (kr[None] - qr[:, None] + 7) * 31 + (kc[None] - qc[:, None] + 15)
        out[t] = np.where(ok, idx, -1)
    return out


def layouts(a):
    L = DEPTH
    f = np.float32
    blocked = lambda w: w.reshape(L, -1, P, w.shape[2] // 512, 512)
    src = {"mod": blocked(a["w_mod"]), "w_in": blocked(a["w_in"]), "br_a": blocked(a["w_br_a"]),
           "br_b": blocked(a["w_br_b"]), "w_out": blocked(a["w_out"])}
    w_stream = np.empty((L, NU, P, 2, 512), f)
    for u, (kind, c, k) in enumerate(UNITS):
        w_stream[:, u] = src[kind][:, 2 * k:2 * k + 2, :, c].transpose(0, 2, 1, 3)
    w_moe = np.empty((L, N_EXP, MU, P, 2, 512), f)
    gu = np.concatenate([a["w_gate"], a["w_up"]], axis=3).reshape(L, N_EXP, 4, 2, P, 512)
    w_moe[:, :, 0:4] = gu.transpose(0, 1, 2, 4, 3, 5)
    w_moe[:, :, 4:6] = a["w_down"].reshape(L, N_EXP, 2, P, 2, 512)
    latents = a["x_sample"][0].reshape(ROWS, GRID_W, D).transpose(1, 0, 2).reshape(4, P, D)
    x_in = np.concatenate([a["x_prompt"], latents]).transpose(1, 0, 2)
    c_cols = np.stack([a["c_ctx"], a["c"][0]]).reshape(2, KC, P).transpose(2, 1, 0)
    lam0 = [0.8 - 0.6 * float(np.exp(-0.3 * l)) for l in range(L)]
    extra = np.array([[v, 1.0 - v] for v in lam0], f)
    params = np.concatenate([a["g_q_da"], a["g_k_da"], a["g_q_na"], a["g_k_na"], a["lam_q1"], a["lam_q2"],
                             a["lam_k1"], a["lam_k2"], a["g_subln"], extra], axis=1)
    b_mod2 = np.stack([a["b_mod"], a["b_mod"]], axis=1)
    g_norms = np.stack([a["g_norm1"], a["g_norm2"]])
    da_k = a["cache_da_k"][0].reshape(L, 2, 2, 2, P, HD)
    da_kc = da_k.transpose(0, 3, 5, 1, 2, 4).reshape(L, P, 4, P)
    da_vc = a["cache_da_v"][0].transpose(0, 2, 1, 3).reshape(L, P, 512)
    na_k = a["cache_na_k"][0].reshape(L, 4, 2, P, HD)
    na_kc = na_k.transpose(0, 2, 4, 1, 3).reshape(L, P, 4, P)
    na_vc = a["cache_na_v"][0].transpose(0, 2, 1, 3).reshape(L, P, 512)
    idx = bias_index()
    rpb = a["rpb"].reshape(L, NA_HEADS, -1)
    full = np.where(idx >= 0, rpb[:, :, np.maximum(idx, 0)], f(NEG))
    bias = np.zeros((L, 4, 4, P, 2, WKEYS), f)
    bias[..., 0:WIN] = full.reshape(L, 4, 2, 4, P, WIN).transpose(0, 3, 1, 4, 2, 5)
    wrt = a["w_router"].reshape(KC, P, N_EXP).transpose(1, 0, 2)
    consts = np.zeros((3, P, P), f)
    consts[0] = np.eye(P)
    consts[1] = np.arange(P)[:, None] < np.arange(P)[None]
    consts[2, :, 0:N_EXP] = np.arange(N_EXP)
    consts[2, :, N_EXP:N_EXP + MOE_TILES] = np.arange(MOE_TILES)
    consts[2, :, N_EXP + MOE_TILES:N_EXP + MOE_TILES + NT] = np.arange(P)[:, None] + P * np.arange(NT)[None]
    tok = np.arange(4 * P)
    pos = np.stack([tok % ROWS, tok // ROWS], axis=-1).astype(f)
    freq = np.power(f(10000.0), -np.arange(16, dtype=f) / f(16), dtype=f)
    ang = pos[:, :, None] * freq
    cos, sin = np.cos(ang), np.sin(ang)
    rope = np.stack([np.stack([cos, cos], axis=2), np.stack([-sin, sin], axis=2)])
    rope = rope.reshape(2, 4, P, HD).transpose(0, 2, 1, 3)
    return {"w_stream": w_stream, "w_moe": w_moe, "x_in": x_in, "c_cols": c_cols, "params": params,
            "b_mod2": b_mod2, "g_norms": g_norms, "da_kc": da_kc, "da_vc": da_vc, "na_kc": na_kc, "na_vc": na_vc,
            "na_bias": bias.reshape(L, 16, P, 2, WKEYS), "w_router": wrt, "b_router": a["b_router"],
            "consts": consts, "rope": rope}


def kernel(**inputs):
    import concourse.bacc as bacc
    from concourse.bass_utils import run_bass_kernel_spmd

    nc = bacc.Bacc("TRN2", target_bir_lowering=False, num_devices=1)
    arrays = {n: np.ascontiguousarray(v, dtype=v.dtype) for n, v in
              layouts({n: np.asarray(v) for n, v in inputs.items()}).items()}
    args = [nc.dram_tensor(n, arrays[n].shape, mybir.dt.from_np(arrays[n].dtype), kind="ExternalInput").ap()
            for n in _RUN_INS]
    outs = {"y_out": (P, NT, D), "dk_out": (1, DEPTH, 2, DA_HEADS, P, HD), "dv_out": (1, DEPTH, DA_HEADS, P, 2 * HD),
            "nk_out": (1, DEPTH, NA_HEADS, P, HD), "nv_out": (1, DEPTH, NA_HEADS, P, HD)}
    args += [nc.dram_tensor(n, shape, F32, kind="ExternalOutput").ap() for n, shape in outs.items()]
    program(nc, *args)
    got = run_bass_kernel_spmd(nc, [arrays], core_ids=[0]).results[0]
    y = np.asarray(got["y_out"]).transpose(1, 0, 2)
    latents = y[1:].reshape(GRID_W, ROWS, D).transpose(1, 0, 2).reshape(1, ROWS * GRID_W, D)
    return (y[0:1], latents, got["dk_out"], got["dv_out"], got["nk_out"], got["nv_out"])
```
